# Optimizing a Trainium2 kernel written in Bass

```python
import math
import jax
import jax.numpy as jnp
from jax import lax
import numpy as np

D_MODEL = 1024
BATCH = 1
SEQ = 256
DEPTH = 2

GRID_W = 64
CTX_LEN = 256
EPS = 1e-6
N_MOD = 9
FFN_HIDDEN = 2816

DA_HEADS = 4
DA_DH = 64
DA_DV = 2 * DA_DH
DA_WIDTH = DA_HEADS * DA_DV
Q_BLOCK = 128
ROPE_BASE = 10000.0
ROPE_PAIRS = DA_DH // 4

HY_WIDTH = 256
HY_ORDER = 2
HY_EMB = 33
HY_BANDS = (HY_EMB - 1) // 2
HY_FILTER_HIDDEN = 64
HY_FAST_DECAY = 0.3
HY_SLOW_DECAY = 1.5
HY_TARGET = 1e-2

SG_WIDTH = 256
SG_GROUPS = 4
SG_CHUNK = 128

N_BRANCH = 3
MIX_WIDTH = DA_WIDTH + HY_WIDTH + SG_WIDTH
HY_OFF = 3 * DA_WIDTH
SG_OFF = HY_OFF + (HY_ORDER + 1) * HY_WIDTH
IN_WIDTH = SG_OFF + 2 * SG_WIDTH

kernel_name = 'hybrid_diffattn_hyena_gmlp_macaron_dit'

def rms_norm(x, gain):
    xf = x.astype(jnp.float32)
    y = xf * lax.rsqrt(jnp.mean(xf * xf, axis=-1, keepdims=True) + EPS)
    return (y * gain.astype(jnp.float32)).astype(x.dtype)

def layer_norm(x, gain, bias):
    xf = x.astype(jnp.float32)
    mu = jnp.mean(xf, axis=-1, keepdims=True)
    var = jnp.mean(jnp.square(xf - mu), axis=-1, keepdims=True)
    y = (xf - mu) * lax.rsqrt(var + EPS)
    return (y * gain.astype(jnp.float32) + bias.astype(jnp.float32)).astype(x.dtype)

def adaln_input(x, mod, i, gain):
    shift = mod[:, 3 * i][:, None]
    scale = mod[:, 3 * i + 1][:, None]
    return rms_norm(x, gain) * (1.0 + scale) + shift

def adaln_gate(mod, i):
    return mod[:, 3 * i + 2][:, None]

def macaron_ffn(xs, mod, i, gain, w_up, w_down):
    h = adaln_input(xs, mod, i, gain)
    a, b = jnp.split(h @ w_up, 2, axis=-1)
    return xs + 0.5 * adaln_gate(mod, i) * ((jax.nn.silu(a) * b) @ w_down)

def axial_rope_tables(n_tokens):
    rows = n_tokens // GRID_W
    row = jnp.repeat(jnp.arange(rows), GRID_W)
    col = jnp.tile(jnp.arange(GRID_W), rows)
    inv = ROPE_BASE ** (-jnp.arange(ROPE_PAIRS, dtype=jnp.float32) / ROPE_PAIRS)
    ang = jnp.stack([row, col], axis=-1).astype(jnp.float32)[:, :, None] * inv
    return jnp.cos(ang), jnp.sin(ang)

def apply_rope(x, cos, sin):
    shp = x.shape
    xr = x.reshape(shp[:-1] + (2, 2, ROPE_PAIRS))
    x1, x2 = xr[..., 0, :], xr[..., 1, :]
    c = cos[None, :, None, None].astype(x.dtype)
    s = sin[None, :, None, None].astype(x.dtype)
    out = jnp.stack([x1 * c - x2 * s, x1 * s + x2 * c], axis=-2)
    return out.reshape(shp)

def split_qkv(proj, qk_gain):
    b, n = proj.shape[:2]
    q = proj[..., :DA_WIDTH].reshape(b, n, DA_HEADS, 2, DA_DH)
    k = proj[..., DA_WIDTH:2 * DA_WIDTH].reshape(b, n, DA_HEADS, 2, DA_DH)
    v = proj[..., 2 * DA_WIDTH:3 * DA_WIDTH].reshape(b, n, DA_HEADS, DA_DV)
    return rms_norm(q, qk_gain[0]), rms_norm(k, qk_gain[1]), v

def diff_softmax_attend(q, k, v, lam):
    s = jnp.einsum('bqhcd,bkhcd->bhcqk', q, k).astype(jnp.float32) * (DA_DH ** -0.5)
    p = jax.nn.softmax(s, axis=-1)
    a = (p[:, :, 0] - lam * p[:, :, 1]).astype(v.dtype)
    return jnp.einsum('bhqk,bkhe->bqhe', a, v)

def diff_attention(pl, pc, cos, sin, qk_gain, lam_vecs, subln, layer_idx, with_ctx):
    lam_init = 0.8 - 0.6 * math.exp(-0.3 * layer_idx)
    lv = lam_vecs.astype(jnp.float32)
    lam = jnp.exp(jnp.sum(lv[0] * lv[1])) - jnp.exp(jnp.sum(lv[2] * lv[3])) + lam_init
    ql, kl, vl = split_qkv(pl, qk_gain)
    qc, kc, vc = split_qkv(pc, qk_gain)
    ql = apply_rope(ql, cos, sin)
    kl = apply_rope(kl, cos, sin)
    k_all = jnp.concatenate([kc, kl], axis=1)
    v_all = jnp.concatenate([vc, vl], axis=1)
    b, n = pl.shape[:2]
    nb = n // Q_BLOCK
    qb = ql.reshape(b, nb, Q_BLOCK, DA_HEADS, 2, DA_DH).swapaxes(0, 1)
    ol = lax.map(lambda qi: diff_softmax_attend(qi, k_all, v_all, lam), qb)
    ol = ol.swapaxes(0, 1).reshape(b, n, DA_HEADS, DA_DV)

    def head_out(o):
        return (rms_norm(o, subln) * (1.0 - lam_init)).reshape(o.shape[0], o.shape[1], DA_WIDTH)

    yl = head_out(ol)
    yc = head_out(diff_softmax_attend(qc, kc, vc, lam)) if with_ctx else None
    return yl, yc

def short_conv(u, w, b):
    up = jnp.pad(u, ((0, 0), (1, 1), (0, 0)))
    return up[:, :-2] * w[0] + up[:, 1:-1] * w[1] + up[:, 2:] * w[2] + b

def hyena_filters(n, w1, b1, w2, b2, freq, w3):
    f32 = jnp.float32
    t = jnp.linspace(0.0, 1.0, n, dtype=f32)[:, None]
    w = (2.0 * math.pi / n) * jnp.arange(n, dtype=f32)[:, None]
    bands = jnp.linspace(1e-4, HY_BANDS - 1, HY_BANDS, dtype=f32)
    z = jnp.concatenate([t, jnp.cos(bands * w), -jnp.sin(bands * w)], axis=-1)
    h = jnp.sin(freq * (z @ w1 + b1))
    h = jnp.sin(freq * (h @ w2 + b2))
    h = (h @ w3).astype(f32).reshape(n, 2, HY_ORDER, HY_WIDTH)
    max_decay = math.log(HY_TARGET) / HY_FAST_DECAY
    min_decay = math.log(HY_TARGET) / HY_SLOW_DECAY
    deltas = jnp.linspace(min_decay, max_decay, HY_ORDER * HY_WIDTH, dtype=f32).reshape(HY_ORDER, HY_WIDTH)
    h = h * jnp.exp(-t[:, :, None] * jnp.abs(deltas))[:, None]
    filt = jnp.concatenate([h[:, 0], jnp.zeros((1, HY_ORDER, HY_WIDTH), f32), jnp.flip(h[1:, 1], axis=0)], axis=0)
    return filt / jnp.sum(jnp.abs(filt), axis=0, keepdims=True)

def bidir_fftconv(u, filt, bias):
    n = u.shape[1]
    uf = jnp.fft.rfft(u.astype(jnp.float32), n=2 * n, axis=1)
    ff = jnp.fft.rfft(filt, n=2 * n, axis=0)
    y = jnp.fft.irfft(uf * ff[None], n=2 * n, axis=1)[:, :n]
    return (y + u.astype(jnp.float32) * bias).astype(u.dtype)

def hyena_branch(proj, conv_w, conv_b, filt_params, skip):
    n = proj.shape[1]
    u = short_conv(proj, conv_w, conv_b)
    v, x1, x2 = jnp.split(u, 3, axis=-1)
    filt = hyena_filters(n, *filt_params)
    z = x1 * bidir_fftconv(v, filt[:, 0], skip[0])
    return x2 * bidir_fftconv(z, filt[:, 1], skip[1])

def sgu_branch(proj, ln_g, ln_b, w_s, b_s):
    b, n = proj.shape[:2]
    u, v = jnp.split(jax.nn.gelu(proj, approximate=False), 2, axis=-1)
    v = layer_norm(v, ln_g, ln_b)
    v = v.reshape(b, n // SG_CHUNK, SG_CHUNK, SG_GROUPS, SG_WIDTH // SG_GROUPS)
    v = jnp.einsum('gij,bnjgc->bnigc', w_s, v) + jnp.transpose(b_s)[None, None, :, :, None]
    return u * v.reshape(b, n, SG_WIDTH)

def merge_branches(h, ya, yb, yc, gate_w, gate_b, w_br, w_o):
    ga, gb, gc = jnp.split(jax.nn.sigmoid(h @ gate_w + gate_b), N_BRANCH, axis=-1)
    m = (ga * (ya @ w_br[:DA_WIDTH])
         + gb * (yb @ w_br[DA_WIDTH:DA_WIDTH + HY_WIDTH])
         + gc * (yc @ w_br[DA_WIDTH + HY_WIDTH:]))
    return m @ w_o

def setup_inputs(seed: int = 0) -> dict:
    key = jax.random.key(seed)
    ks = iter(jax.random.split(key, 32))
    f32 = jnp.float32

    def nrm(shape, scale):
        return jax.random.normal(next(ks), shape, f32) * scale

    L = DEPTH
    return {
        'x': nrm((BATCH, SEQ, D_MODEL), 1.0),
        'c': nrm((BATCH, D_MODEL), 1.0),
        'ctx': nrm((BATCH, CTX_LEN, D_MODEL), 1.0),
        'c_ctx': nrm((D_MODEL,), 1.0),
        'ada_w': nrm((L, D_MODEL, N_MOD * D_MODEL), D_MODEL ** -0.5),
        'ada_b': nrm((L, N_MOD * D_MODEL), 0.02),
        'norm_g': 1.0 + nrm((L, 3, D_MODEL), 0.02),
        'ffn_up': nrm((L, 2, D_MODEL, 2 * FFN_HIDDEN), D_MODEL ** -0.5),
        'ffn_down': nrm((L, 2, FFN_HIDDEN, D_MODEL), FFN_HIDDEN ** -0.5),
        'w_in': nrm((L, D_MODEL, IN_WIDTH), D_MODEL ** -0.5),
        'da_qk_gain': 1.0 + nrm((L, 2, DA_DH), 0.02),
        'da_lambda': nrm((L, 4, DA_DH), 0.1),
        'da_subln': 1.0 + nrm((L, DA_DV), 0.02),
        'hy_conv_w': nrm((L, 3, (HY_ORDER + 1) * HY_WIDTH), 0.5),
        'hy_conv_b': nrm((L, (HY_ORDER + 1) * HY_WIDTH), 0.02),
        'hy_f_w1': nrm((L, HY_EMB, HY_FILTER_HIDDEN), HY_EMB ** -0.5),
        'hy_f_b1': nrm((L, HY_FILTER_HIDDEN), 0.1),
        'hy_f_w2': nrm((L, HY_FILTER_HIDDEN, HY_FILTER_HIDDEN), HY_FILTER_HIDDEN ** -0.5),
        'hy_f_b2': nrm((L, HY_FILTER_HIDDEN), 0.1),
        'hy_f_freq': 1.0 + nrm((L, HY_FILTER_HIDDEN), 0.05),
        'hy_f_w3': nrm((L, HY_FILTER_HIDDEN, 2 * HY_ORDER * HY_WIDTH), HY_FILTER_HIDDEN ** -0.5),
        'hy_skip': nrm((L, HY_ORDER, HY_WIDTH), 0.5),
        'sg_ln_g': 1.0 + nrm((L, SG_WIDTH), 0.02),
        'sg_ln_b': nrm((L, SG_WIDTH), 0.02),
        'sg_w': nrm((L, SG_GROUPS, SG_CHUNK, SG_CHUNK), SG_CHUNK ** -0.5),
        'sg_b': 1.0 + nrm((L, SG_GROUPS, SG_CHUNK), 0.02),
        'gate_w': nrm((L, D_MODEL, N_BRANCH * D_MODEL), D_MODEL ** -0.5),
        'gate_b': nrm((L, N_BRANCH * D_MODEL), 0.02),
        'w_br': nrm((L, MIX_WIDTH, D_MODEL), DA_WIDTH ** -0.5),
        'w_o': nrm((L, D_MODEL, D_MODEL), D_MODEL ** -0.5),
    }

def reference(x, c, ctx, c_ctx, ada_w, ada_b, norm_g, ffn_up, ffn_down, w_in, da_qk_gain, da_lambda, da_subln,
              hy_conv_w, hy_conv_b, hy_f_w1, hy_f_b1, hy_f_w2, hy_f_b2, hy_f_freq, hy_f_w3, hy_skip,
              sg_ln_g, sg_ln_b, sg_w, sg_b, gate_w, gate_b, w_br, w_o):
    cos, sin = axial_rope_tables(x.shape[1])
    s_lat = jax.nn.silu(c)
    s_ctx = jax.nn.silu(c_ctx)[None]
    xl, xc = x, ctx
    for l in range(DEPTH):
        last = l == DEPTH - 1
        mod_l = (s_lat @ ada_w[l] + ada_b[l]).reshape(-1, N_MOD, D_MODEL)
        mod_c = (s_ctx @ ada_w[l] + ada_b[l]).reshape(1, N_MOD, D_MODEL)

        xl = macaron_ffn(xl, mod_l, 0, norm_g[l, 0], ffn_up[l, 0], ffn_down[l, 0])
        xc = macaron_ffn(xc, mod_c, 0, norm_g[l, 0], ffn_up[l, 0], ffn_down[l, 0])

        hl = adaln_input(xl, mod_l, 1, norm_g[l, 1])
        hc = adaln_input(xc, mod_c, 1, norm_g[l, 1])
        pl = hl @ w_in[l]
        pc = hc @ w_in[l]
        filt_params = (hy_f_w1[l], hy_f_b1[l], hy_f_w2[l], hy_f_b2[l], hy_f_freq[l], hy_f_w3[l])
        ya_l, ya_c = diff_attention(pl, pc, cos, sin, da_qk_gain[l], da_lambda[l], da_subln[l], l, not last)
        yb_l = hyena_branch(pl[..., HY_OFF:SG_OFF], hy_conv_w[l], hy_conv_b[l], filt_params, hy_skip[l])
        yc_l = sgu_branch(pl[..., SG_OFF:], sg_ln_g[l], sg_ln_b[l], sg_w[l], sg_b[l])
        xl = xl + adaln_gate(mod_l, 1) * merge_branches(hl, ya_l, yb_l, yc_l, gate_w[l], gate_b[l], w_br[l], w_o[l])

        xl = macaron_ffn(xl, mod_l, 2, norm_g[l, 2], ffn_up[l, 1], ffn_down[l, 1])

        if not last:
            yb_c = hyena_branch(pc[..., HY_OFF:SG_OFF], hy_conv_w[l], hy_conv_b[l], filt_params, hy_skip[l])
            yc_c = sgu_branch(pc[..., SG_OFF:], sg_ln_g[l], sg_ln_b[l], sg_w[l], sg_b[l])
            xc = xc + adaln_gate(mod_c, 1) * merge_branches(hc, ya_c, yb_c, yc_c, gate_w[l], gate_b[l], w_br[l], w_o[l])
            xc = macaron_ffn(xc, mod_c, 2, norm_g[l, 2], ffn_up[l, 1], ffn_down[l, 1])
    return xl


_drawn_inputs = setup_inputs


def setup_inputs(seed=0):
    import zlib

    import numpy as np

    out = dict(_drawn_inputs(seed))
    spreads = {}
    factors = {'norm_g': 2.926,
     'da_qk_gain': 8.0,
     'da_subln': 30.92,
     'hy_conv_b': 8.0,
     'hy_f_b1': 4.54,
     'hy_f_b2': 3.886,
     'hy_f_freq': 8.0,
     'sg_ln_g': 8.0,
     'sg_ln_b': 8.0,
     'sg_b': 8.0,
     'gate_b': 8.0}
    for name, (base, spread) in spreads.items():
        noise = np.random.default_rng([zlib.crc32(name.encode()), seed]).standard_normal(out[name].shape)
        drawn = base * np.exp(spread * noise) if base else spread * noise
        out[name] = jnp.asarray(drawn.astype(out[name].dtype))
    for name, factor in factors.items():
        out[name] = (out[name] * factor).astype(out[name].dtype)
    return out
```

```python
from contextlib import ExitStack
import math

import numpy as np

import concourse.bass as bass
from concourse import mybir

F32 = mybir.dt.float32
F32R = mybir.dt.float32r
ACT = mybir.ActivationFunctionType
ALU = mybir.AluOpType
AX = mybir.AxisListType

P = 128
D = 1024
KD = D // P
SEQ = 256
TOK = 512
NT = TOK // P
DEPTH = 2
N_MOD = 9
FFN = 2816
KF = FFN // P
EPS = 1e-6

HEADS, DH, DV = 4, 64, 128
DA = HEADS * DV
HYW = 256
SGW = 256
HY_OFF = 3 * DA
SG_OFF = HY_OFF + 3 * HYW
GRID_W = 64
EMB, FH = 33, 64

SLOTS = 4
LOOK = 3
UP_GROUPS = FFN // 256
DOWN_PAIRS = KF // 2
FFN_PAIRS = 4 * UP_GROUPS + 2 * DOWN_PAIRS
ADA_GROUPS = N_MOD * D // 512
ADA_START = 7
COLS_A, COLS_B = 120, 32


def lam_init(layer):
    return 0.8 - 0.6 * math.exp(-0.3 * layer)


def up_tiles():
    return (0, 256, 128, 384)


def banks_of(group):
    return (0, 1, 2, 3) if group % 2 == 0 else (4, 5, 6, 3)


class Chain:

    def __init__(self, eng, sem):
        self.eng, self.sem, self.n = eng, sem, 0

    def step(self, ins):
        self.n += 1
        return ins.then_inc(self.sem, 1)

    def after(self, back=0):
        self.eng.wait_ge(self.sem, self.n - back)



def mix_gemms(layer):
    out = [("k", "w_in", 0, DA, 4, 512), ("q", "w_in", 0, 0, 4, 512), ("v", "w_in", 0, 2 * DA, 4, 512),
           ("sgv", "w_in", 0, SG_OFF + SGW, 4, 256),
           ("f0", "w_in", 0, HY_OFF, 4, 512), ("f1", "w_in", 0, HY_OFF + 512, 4, 512)]
    for branch, gate, row, pairs in (("c", 2, DA + HYW, 1), ("b", 1, DA, 1), ("a", 0, 0, 2)):
        for g in range(2):
            out.append((f"gate_{branch}{g}", "gate_w", 0, gate * D + g * 512, 4, 512))
            out.append((f"br_{branch}{g}", "w_br", row, g * 512, pairs, 512))
    out += [(f"o{g}", "w_o", 0, g * 512, 4, 512) for g in range(2)]
    return out


MIX_PAIRS = sum(g[4] for g in mix_gemms(0))


def softmax_units(streams):
    units = [((qc,), 0, h) for qc in range(2) for h in range(HEADS)]
    if streams == 2:
        units += [((2, 3), 2, h) for h in range(HEADS)]
    return units


def mix_schedule(streams):
    units = softmax_units(streams)
    attention = [[("scores", 0)]]
    for u in range(len(units)):
        attention.append([("turn", u)])
        attention.append([("mixv", u)] + ([("scores", u + 1)] if u + 1 < len(units) else []))
    hyena = []
    for order in range(2):
        hyena += [[("h_turn", order)]]
        for s in range(streams):
            hyena += [[("h_fwd", order, s)], [("h_inv", order, s)]]
    gaps = [[("ws_turn",), ("qk_turn", 0)], [("qk_turn", 1), ("qk_turn", 2)], [("qk_turn", 3), ("sg_mix",)]]
    while attention or hyena:
        gaps.append((attention.pop(0) if attention else []) + (hyena.pop(0) if hyena else []))
    tail = [("y_turn", c) for c in range(streams)]
    order = []
    for name, _, _, _, pairs, _ in mix_gemms(0)[6:-2]:
        assert name != "br_b0" or not any(x[0][0] == "h" or x[-1][0][0] == "h" for x in gaps)
        if name == "br_a0":
            for step in gaps:
                order += step
            gaps = []
            order += tail
        for j in range(pairs):
            order.append(("pair", name, j))
            if j == pairs - 1:
                order.append(("drain", name))
            if gaps:
                order += gaps.pop(0)
    return order


def small_products(schedule):
    names = [s for s in schedule if s[0] not in ("pair", "drain")]
    return {s: n for n, s in enumerate(names)}



def build(nc, t, out):
    ctx = ExitStack()
    with ctx:
        place_at = [16640]

        def sb(name, shape, dt=F32, at=None):
            size = -(-math.prod(shape[1:]) * 4 // 32) * 32
            where = place_at[0] if at is None else at
            if at is None:
                place_at[0] += size
            assert where + size <= 229344, (name, where + size)
            return nc.alloc_sbuf_tensor_at(name, shape, dt, offset=where)

        def sem(name):
            return ctx.enter_context(nc.semaphore(name))

        x = sb("x", [P, KD, TOK])
        h_hi = sb("h_hi", [P, KD, TOK], F32R)
        h_lo_at = place_at[0]
        h_lo = sb("h_lo", [P, KD, TOK], F32R)
        raw = sb("raw", [P, SLOTS, 1024])
        w_hi = sb("w_hi", [P, SLOTS, 1024], F32R)
        w_lo = sb("w_lo", [P, SLOTS, 1024], F32R)
        ident = sb("ident", [P, P])
        ones = sb("ones", [P, P])
        prm = sb("prm", [P, DEPTH, COLS_A + COLS_B])
        mod = sb("mod", [P, DEPTH, N_MOD * KD, 2])
        mod_a = sb("mod_a", [P, 3 * DEPTH, KD, 2])
        mod_g = sb("mod_g", [P, 3 * DEPTH, KD, 2])
        sil_c = sb("sil_c", [P, KD, 2])
        lam = sb("lam", [P, DEPTH])
        half_pow = sb("half_pow", [P, 64])
        ms = sb("ms", [P, 64])
        rstd = sb("rstd", [P, 64])
        arena = place_at[0]

        u_hi = sb("u_hi", [P, KF, TOK], F32R)
        u_lo = sb("u_lo", [P, KF, TOK], F32R)
        ada_raw = sb("ada_raw", [P, 2, 1024])
        ada_acc = sb("ada_acc", [P, 2, 512])
        uf = sb("uf", [P, 2, TOK])
        ffn_end = place_at[0]
        sq_h = sb("sq_h", [P, KD, TOK], at=h_lo_at)
        sq_m = sb("sq_m", [P, KD, TOK], at=arena)
        hf = sb("hf", [P, 3, TOK], at=arena)
        diag = sb("diag", [P, TOK], at=arena + 6144)
        y_out = sb("y_out", [P, 2, D], at=arena)

        place_at[0] = arena + 8192
        ada0 = sb("ada0", [P, 3, KD * 512])
        zt = sb("zt", [EMB, SEQ])
        fw1 = sb("fw1", [EMB, DEPTH, FH])
        fw2 = sb("fw2", [FH, DEPTH, FH])
        fw3 = sb("fw3", [FH, DEPTH, 1024])
        f_arg = sb("f_arg", [FH, SEQ])
        f_turns = sb("f_turns", [FH, SEQ])
        f_sin = sb("f_sin", [FH, 2, SEQ])
        dft_f0 = sb("dft_f0", [P, 2, 2, SEQ])
        decay = sb("decay", [P, 2, 2, 512])
        taps = sb("taps", [P, 2, 2, 512])
        tmag = sb("tmag", [P, 2, 2, 512])
        inv_l1 = sb("inv_l1", [P, 512])
        prow = sb("prow", [P, DEPTH, 2, P])
        crow = sb("crow", [2 * KD, P])
        lv = sb("lv", [P, DEPTH, 4, DH])
        lsum = sb("lsum", [P, 2 * DEPTH])
        scol = sb("scol", [P, 2 * KD])
        spec0 = taps
        start_end = place_at[0]

        place_at[0] = arena
        r1 = place_at[0]
        qk = sb("qk", [P, NT, 1024])
        dft = sb("dft", [P, 2, 2, 2, SEQ], at=r1)
        spec = sb("spec", [P, 2, 2, 512], at=r1 + 8192)
        ya_hi = sb("ya_hi", [P, HEADS, TOK], F32R, at=r1)
        ya_lo = sb("ya_lo", [P, HEADS, TOK], F32R, at=r1 + 8192)
        vtok = sb("vtok", [P, NT, DA])
        qT = sb("qT", [P, HEADS, TOK])
        kT = sb("kT", [P, HEADS, TOK])
        e_at = place_at[0]
        e = sb("e", [P, 2, 512])
        tmp = sb("tmp", [P, 1024], at=e_at)
        aT = sb("aT", [P, 512])
        gate_at = place_at[0]
        gate = sb("gate", [P, 4, TOK])
        ws = sb("ws", [P, 4, P], at=gate_at)
        merged = sb("merged", [P, KD, TOK])
        hy_at = place_at[0]
        hy = sb("hy", [P, 6, TOK])
        yb_lo = sb("yb_lo", [P, 2, TOK], F32R, at=hy_at)
        yb_hi = sb("yb_hi", [P, 2, TOK], F32R, at=hy_at + 4096)
        sgu_at = place_at[0]
        sgu = sb("sgu", [P, 2, TOK])
        yc_lo = sb("yc_lo", [P, 2, TOK], F32R, at=sgu_at)
        yc_at = place_at[0]
        yc_hi = sb("yc_hi", [P, 2, TOK], F32R)
        sgv_at = place_at[0]
        sgv = sb("sgv", [P, NT, SGW])
        htok = sb("htok", [P, NT, HYW], at=sgv_at)
        hprod_at = place_at[0]
        hprod = sb("hprod", [P, 2, 2, HYW])
        htmp = sb("htmp", [P, 2, HYW])
        o0 = sb("o0", [P, DA])
        o_tok = [o0, sb("o1", [P, DA], at=yc_at), sb("o2", [P, DA], at=yc_at + 2048),
                 sb("o3", [P, DA], at=sgu_at)]
        rope = sb("rope", [P, 2, 2, 32])
        qk_gain = sb("qk_gain", [P, 2, DH])
        ln_g = sb("ln_g", [P, SGW])
        ln_b = sb("ln_b", [P, SGW])
        sgb = sb("sgb", [P, 2, P])
        wsT = sb("wsT", [P, 4, P], at=hprod_at)
        sm = sb("sm", [P, 16])
        stats = sb("stats", [P, NT, 8])
        mix_end = place_at[0]

        ps = ctx.enter_context(nc.psum_tensor("ps", [P, 8, 512], F32))
        MISC = 7
        spectra = nc.dram_tensor("hyena_spectra", [DEPTH, P, 2 * 2 * 512], F32, kind="Internal").ap()

        raw_loaded = [sem(f"raw_loaded{i}") for i in range(SLOTS)]
        hi_ready = sem("hi_ready")
        lo_ready = sem("lo_ready")
        pair_used = sem("pair_used")
        const_loaded = sem("const_loaded")
        row_loaded = sem("row_loaded")
        row_cleared = sem("row_cleared")
        flt_loaded = sem("flt_loaded")
        ada0_loaded = [sem(f"ada0_loaded{i}") for i in range(3)]
        ones_set = sem("ones_set")
        turned = sem("turned")
        prm_ready = sem("prm_ready")
        sil_ready = sem("sil_ready")
        xt_done = sem("xt_done")
        x0_ready = sem("x0_ready")
        ada0_done = sem("ada0_done")
        ada0_out = sem("ada0_out")
        flt_pe = sem("flt_pe")
        flt_v = sem("flt_v")
        flt_a = sem("flt_a")
        spec_stored = sem("spec_stored")
        lv_loaded = sem("lv_loaded")
        lam_v = sem("lam_v")
        lam_a = sem("lam_a")
        x_ready = sem("x_ready")
        squared = sem("squared")
        sums_done = sem("sums_done")
        ms_ready = sem("ms_ready")
        rstd_ready = sem("rstd_ready")
        diag_ready = sem("diag_ready")
        rstd_spread = sem("rstd_spread")
        hf_step = sem("hf_step")
        h_hi_ready = sem("h_hi_ready")
        h_ready = sem("h_ready")
        mod_step = sem("mod_step")
        tile_done = [sem(f"tile_done{f}") for f in range(4)]
        sil_a = sem("sil_a")
        uf_ready = sem("uf_ready")
        u_hi_ready = sem("u_hi_ready")
        u_ready = sem("u_ready")
        ada_loaded = [sem(f"ada_loaded{i}") for i in range(2)]
        ada_step = sem("ada_step")
        ada_folded = sem("ada_folded")
        ada_taken = sem("ada_taken")
        def by_layer(name):
            return [sem(f"{name}_{layer}") for layer in range(DEPTH)]

        mix_done = by_layer("mix_done")
        drained = [{g[0]: sem(f"drained_{g[0]}_{layer}") for g in mix_gemms(layer)[:-2]} for layer in range(DEPTH)]
        small_done = by_layer("small_done")
        slot_free = [[sem(f"slot_free{b}_{layer}") for b in range(2)] for layer in range(DEPTH)]
        mixc_loaded = by_layer("mixc_loaded")
        dft_loaded = by_layer("dft_loaded")
        conv_ready = by_layer("conv_ready")
        z_ready = by_layer("z_ready")
        qk_normed = by_layer("qk_normed")
        ln_done = by_layer("ln_done")
        ws_ready = by_layer("ws_ready")
        qkT_ready = by_layer("qkT_ready")
        yc_full = by_layer("yc_full")
        yc_hi_ready = by_layer("yc_hi_ready")
        yc_ready = by_layer("yc_ready")
        yb_full = by_layer("yb_full")
        yb_hi_ready = by_layer("yb_hi_ready")
        yb_ready = by_layer("yb_ready")
        ya_hi_ready = by_layer("ya_hi_ready")
        ya_ready = by_layer("ya_ready")
        htok_ready = by_layer("htok_ready")
        hprod_ready = by_layer("hprod_ready")
        max_ready = by_layer("max_ready")
        exp_ready = by_layer("exp_ready")
        a_ready = by_layer("a_ready")
        aT_ready = by_layer("aT_ready")
        o_ready = by_layer("o_ready")
        o_normed = by_layer("o_normed")
        m_hi_ready = by_layer("m_hi_ready")
        m_ready = by_layer("m_ready")
        v_step = sem("v_step")
        out_turned = sem("out_turned")
        out_copied = sem("out_copied")
        out_stored = sem("out_stored")

        ffn_first = []
        mix_first = []
        w = 0
        for layer in range(DEPTH):
            ffn_first.append(w)
            w += FFN_PAIRS
            mix_first.append(w)
            w += MIX_PAIRS
            ffn_first.append(w)
            w += FFN_PAIRS
        N_PAIRS = w
        FFNS = [(0, 0, TOK), (0, 2, TOK), (1, 0, TOK), (1, 2, SEQ)]
        MIX_T = [TOK, SEQ]
        ADA_FFN_GROUPS = [UP_GROUPS, UP_GROUPS, 2 * ADA_GROUPS - ADA_START - 2 * UP_GROUPS, 0]
        ADA_FFN_FIRST = [0, UP_GROUPS, 2 * UP_GROUPS, 0]

        def ada_src(q, k0, k1):
            layer, g = q // ADA_GROUPS, q % ADA_GROUPS
            return t["ada_w"][layer, k0 * P:k1 * P, g * 512:(g + 1) * 512].rearrange("(k p) n -> p k n", p=P)

        def mix_gemm(layer, name):
            w = mix_first[layer]
            for g in mix_gemms(layer):
                if g[0] == name:
                    return w, g
                w += g[4]

        block = ctx.enter_context(nc.Block())

        @block.sync
        def _(sp):
            sp.dma_start(ident[:, :], t["ident"]).then_inc(const_loaded, 16)
            for c in range(NT):
                src = (t["x"][0] if c < 2 else t["ctx"][0])[(c % 2) * P:(c % 2 + 1) * P, :]
                for k in range(2):
                    sp.dma_start(raw[:, c, k * 512:(k + 1) * 512], src[:, k * 512:(k + 1) * 512])\
                        .then_inc(raw_loaded[c], 16)
            for q in range(ADA_START):
                if q >= 3:
                    sp.wait_ge(ada0_done, q - 2)
                sp.dma_start(ada0[:, q % 3, :].rearrange("p (k n) -> p k n", k=KD), ada_src(q, 0, KD))\
                    .then_inc(ada0_loaded[q % 3], 16)

            def load_up(slot, w_up, j, col):
                for k in range(2):
                    rows = w_up[(2 * j + k) * P:(2 * j + k + 1) * P, :].rearrange("p (s n) -> p s n", s=2)
                    sp.dma_start(raw[:, slot, k * 512:(k + 1) * 512].rearrange("p (s n) -> p s n", s=2),
                                 rows[:, :, col]).then_inc(raw_loaded[slot], 16)

            def load_rows(slot, matrix, row, col, cols):
                for k in range(2):
                    sp.dma_start(raw[:, slot, k * 512:k * 512 + cols],
                                 matrix[bass.ds(row + k * P, P), col:col + cols]).then_inc(raw_loaded[slot], 16)

            def load_ffn(f):
                layer, which, w0 = f // 2, f % 2, ffn_first[f]
                w_up, w_down = t["ffn_up"][layer, which], t["ffn_down"][layer, which]
                first = 0
                if f == 0:
                    sp.wait_ge(x0_ready, 2 * NT)
                    for j in range(4):
                        load_up((w0 + j) % SLOTS, w_up, j, slice(0, 256))
                    first = 1
                with sp.Fori(first, UP_GROUPS) as g:
                    for j in range(4):
                        sp.wait_ge(lo_ready, g * 4 + (w0 + j - SLOTS + 1))
                        load_up((w0 + j) % SLOTS, w_up, j, bass.ds(g * 256, 256))
                for half in range(2):
                    wd = w0 + 4 * UP_GROUPS + half * DOWN_PAIRS
                    with sp.Fori(0, DOWN_PAIRS // 4) as i:
                        for j in range(4):
                            sp.wait_ge(lo_ready, i * 4 + (wd + j - SLOTS + 1))
                            load_rows((wd + j) % SLOTS, w_down, i * 1024 + j * 256, half * 512, 512)
                    for j in range(DOWN_PAIRS // 4 * 4, DOWN_PAIRS):
                        sp.wait_ge(lo_ready, wd + j - SLOTS + 1)
                        load_rows((wd + j) % SLOTS, w_down, j * 256, half * 512, 512)

            def load_mix(layer):
                w = mix_first[layer]
                for _, weight, row, col, pairs, cols in mix_gemms(layer):
                    for j in range(pairs):
                        sp.wait_ge(lo_ready, w - SLOTS + 1)
                        load_rows(w % SLOTS, t[weight][layer], row + j * 256, col, cols)
                        w += 1

            for layer in range(DEPTH):
                load_ffn(2 * layer)
                load_mix(layer)
                load_ffn(2 * layer + 1)
            for c in range(2):
                sp.wait_ge(out_copied, 2 * c + 2)
                sp.dma_start(out[c * P:(c + 1) * P, :], y_out[:, c, :]).then_inc(out_stored, 16)
            sp.wait_ge(out_stored, 32)

        SCHED = [mix_schedule(T // SEQ) for T in MIX_T]
        SMALL = [small_products(s) for s in SCHED]
        UNITS = [softmax_units(T // SEQ) for T in MIX_T]
        GEMM_AT = {g[0]: n for n, g in enumerate(mix_gemms(0))}
        N_CHUNKS = [T // P for T in MIX_T]
        N_ROWS = 2 + 10 * DEPTH

        def in_tiles(layer, name):
            if name in ("q", "sgv"):
                return N_CHUNKS[layer]
            return 4

        def tiles_before(layer, name):
            n = 0
            for g in mix_gemms(layer):
                if g[0] == name:
                    return n
                n += in_tiles(layer, g[0])

        def power_request(layer, what):
            return 6 * layer + ("ffn_a", "mix", "qk", "ln", "head", "ffn_b").index(what)

        FLT_V, FLT_P, FLT_A = 22, 6, 4

        def HF_FULL(n, k):
            return 24 * n + (3 if n < 5 else 2) * (k + 1)

        def pair_cols(w):
            for layer in range(DEPTH):
                first = mix_gemm(layer, "sgv")[0]
                if first <= w < first + 4:
                    return SGW
            return 512

        @block.gpsimd
        def _(pool):
            pool.memset(prow[:, :, :, :], 0.0).then_inc(row_cleared, 1)
            pool.memset(ones[:, :], 1.0).then_inc(ones_set, 1)
            pool.memset(half_pow[:, :], -0.5).then_inc(ones_set, 1)
            pool.dma_start(zt[:, :], t["filter_pos"]).then_inc(flt_loaded, 16)
            pool.dma_start(fw1[:, :, :], t["hy_f_w1"].rearrange("l a b -> a l b")).then_inc(flt_loaded, 16)
            pool.dma_start(fw2[:, :, :], t["hy_f_w2"].rearrange("l a b -> a l b")).then_inc(flt_loaded, 16)
            pool.dma_start(fw3[:, :, :], t["hy_f_w3"].rearrange("l a b -> a l b")).then_inc(flt_loaded, 16)
            pool.dma_start(decay[:, :, :, :].rearrange("p c a b -> p c (a b)"),
                           t["decay"].rearrange("(c p) a b -> p c (a b)", p=P)).then_inc(flt_loaded, 16)
            pool.dma_start(dft_f0[:, :, :, :].rearrange("p c a b -> p c (a b)"),
                           t["dft"][0].rearrange("(c p) a b -> p c (a b)", p=P)).then_inc(flt_loaded, 16)
            pool.wait_ge(ones_set, 2)

            def power(request, cols):
                pool.wait_ge(ms_ready, request + 1)
                pool.tensor_tensor(rstd[:, 0:cols], ms[:, 0:cols], half_pow[:, 0:cols], ALU.pow)\
                    .then_inc(rstd_ready, 1)

            def store_spectrum(layer):
                pool.wait_ge(flt_v, FLT_V * (layer + 1))
                pool.dma_start(spectra[layer], spec0[:, :, :, :].rearrange("p a b c -> p (a b c)"))\
                    .then_inc(spec_stored, 16)

            def load_ada(f):
                first, groups = ADA_FFN_FIRST[f], ADA_FFN_GROUPS[f]
                q0 = ADA_START + first
                runs, q = [], q0
                while q < q0 + groups:
                    stop = min(q0 + groups, (q // ADA_GROUPS + 1) * ADA_GROUPS)
                    runs.append((q, stop))
                    q = stop
                for a, b in runs:
                    w_ada, col = t["ada_w"][a // ADA_GROUPS], (a % ADA_GROUPS) * 512
                    v0 = 4 * (a - ADA_START)

                    def unit(i, j, wait):
                        if wait is not None:
                            pool.wait_ge(ada_step, wait)
                        src = w_ada[2 * j * P:(2 * j + 2) * P, bass.ds(i * 512 + col, 512)]
                        pool.dma_start(ada_raw[:, j % 2, :].rearrange("p (k n) -> p k n", k=2),
                                       src.rearrange("(k p) n -> p k n", p=P)).then_inc(ada_loaded[j % 2], 16)

                    first_run = v0 == 0
                    if first_run:
                        for j in range(4):
                            unit(0, j, 4 * (j - 1) if j >= 2 else None)
                    with pool.Fori(1 if first_run else 0, b - a) as i:
                        for j in range(4):
                            unit(i, j, i * 16 + 4 * (v0 + j - 1))

            def load_mix_constants(layer):
                pool.wait_ge(pair_used, mix_first[layer])
                n = mixc_loaded[layer]
                pool.dma_start(rope[:, :, :, :].rearrange("p c a b -> p c (a b)"),
                               t["rope"].rearrange("(c p) a b -> p c (a b)", p=P)).then_inc(n, 16)
                pool.dma_start(qk_gain[:, :, :], t["da_qk_gain"][layer].partition_broadcast(P)).then_inc(n, 16)
                pool.dma_start(ln_g[:, :], t["sg_ln_g"][layer:layer + 1, :].rearrange("a b -> (a b)")
                               .partition_broadcast(P)).then_inc(n, 16)
                pool.dma_start(ln_b[:, :], t["sg_ln_b"][layer:layer + 1, :].rearrange("a b -> (a b)")
                               .partition_broadcast(P)).then_inc(n, 16)
                for g in range(4):
                    pool.dma_start(sgb[64 * (g % 2):64 * (g % 2) + 64, g // 2, :],
                                   t["sg_b"][layer, g].partition_broadcast(64)).then_inc(n, 16)
                pool.dma_start(ws[:, :, :], t["sg_w"][layer].rearrange("g i j -> i g j")).then_inc(n, 16)

            def load_dft(layer):
                pool.wait_ge(qkT_ready[layer], 4)
                for way in range(2):
                    for c in range(2):
                        pool.dma_start(dft[:, c, way, :, :], t["dft"][way, c * P:(c + 1) * P]).then_inc(dft_loaded[layer], 16)
                pool.wait_ge(spec_stored, 16 * (layer + 1))
                pool.dma_start(spec[:, :, :, :].rearrange("p a b c -> p (a b c)"), spectra[layer])\
                    .then_inc(dft_loaded[layer], 16)

            store_spectrum(0)
            store_spectrum(1)
            for layer in range(DEPTH):
                power(power_request(layer, "ffn_a"), NT)
                load_ada(2 * layer)
                power(power_request(layer, "mix"), NT)
                load_mix_constants(layer)
                power(power_request(layer, "qk"), 64)
                power(power_request(layer, "ln"), NT)
                load_dft(layer)
                power(power_request(layer, "head"), 16)
                power(power_request(layer, "ffn_b"), NT)
                if layer == 0:
                    load_ada(1)

        @block.scalar
        def _(act):
            for layer in range(DEPTH):
                rows = prow[:, layer, 0, :]
                if layer == 0:
                    act.dma_start(crow[0:KD, :], t["c"].rearrange("a (k p) -> (a k) p", p=P)).then_inc(row_loaded, 16)
                    act.dma_start(crow[KD:, :], t["c_ctx"].rearrange("(k p) -> k p", p=P)).then_inc(row_loaded, 16)
                    act.wait_ge(row_cleared, 1)
                act.dma_start(rows[0:72, :], t["ada_b"][layer].rearrange("(r p) -> r p", p=P)).then_inc(row_loaded, 16)
                act.dma_start(rows[72:96, :], t["norm_g"][layer].rearrange("i (k p) -> (i k) p", p=P)).then_inc(row_loaded, 16)
                act.dma_start(rows[96:120, :], t["gate_b"][layer].rearrange("(r p) -> r p", p=P)).then_inc(row_loaded, 16)
                rows = prow[:, layer, 1, :]
                act.dma_start(rows[0:18, :], t["hy_conv_w"][layer].rearrange("i (k p) -> (i k) p", p=P)).then_inc(row_loaded, 16)
                act.dma_start(rows[18:24, :], t["hy_conv_b"][layer].rearrange("(r p) -> r p", p=P)).then_inc(row_loaded, 16)
                act.dma_start(rows[24:28, :], t["hy_skip"][layer].rearrange("i (k p) -> (i k) p", p=P)).then_inc(row_loaded, 16)
                act.dma_start(rows[28:29, :], t["da_subln"][layer:layer + 1, :]).then_inc(row_loaded, 16)
                for i, name in enumerate(("hy_f_b1", "hy_f_b2", "hy_f_freq")):
                    act.dma_start(rows[29 + i:30 + i, 0:FH], t[name][layer:layer + 1, :]).then_inc(row_loaded, 16)
            for layer in range(DEPTH):
                act.dma_start(lv[:, layer, :, :], t["da_lambda"][layer].partition_broadcast(P)).then_inc(lv_loaded, 16)

            act.wait_ge(turned, 1)
            act.activation(sil_c[:, :, :].rearrange("p k s -> p s k"),
                           ps[:, MISC, 0:2 * KD].rearrange("p (s k) -> p s k", s=2), ACT.Silu).then_inc(sil_ready, 1)
            act.wait_ge(lam_v, 2 * DEPTH)
            act.activation(lsum[:, :], lsum[:, :], ACT.Exp).then_inc(lam_a, 1)

            for layer in range(DEPTH):
                v0 = FLT_V * layer
                act.wait_ge(flt_v, v0 + 7)
                act.activation(f_sin[:, 0, :], f_arg[:, :], ACT.Sin).then_inc(flt_a, 1)
                act.wait_ge(flt_v, v0 + 14)
                act.activation(f_sin[:, 1, :], f_arg[:, :], ACT.Sin).then_inc(flt_a, 1)
                for c in range(2):
                    act.wait_ge(flt_v, v0 + 16 + 2 * c)
                    act.activation(tmag[:, c, :, :], taps[:, c, :, :], ACT.Abs).then_inc(flt_a, 1)

            def split_high(w, slot, cols=512, wait=None, free=None):
                act.wait_ge(raw_loaded[slot], wait)
                if free is not None:
                    act.wait_ge(pair_used, free)
                src = raw[:, slot, :].rearrange("p (k n) -> p k n", k=2)[:, :, 0:cols]
                dst = w_hi[:, slot, :].rearrange("p (k n) -> p k n", k=2)[:, :, 0:cols]
                act.activation(dst, src, ACT.Copy).then_inc(hi_ready, 1)

            def split_ahead(w):
                v = w + LOOK
                if v < N_PAIRS:
                    split_high(v, v % SLOTS, pair_cols(v), 32 * (v // SLOTS + 2),
                               v - SLOTS + 1 if v >= SLOTS else None)

            def split_ahead_in_loop(w0, j, turns, i):
                v = w0 + j + LOOK
                split_high(v, v % SLOTS, 512, i * (32 * turns // SLOTS) + 32 * (v // SLOTS + 2),
                           i * turns + (v - SLOTS + 1))

            def norm(n, T, squares):
                for k in range(KD):
                    if n == 0:
                        act.wait_ge(x0_ready, 2 * NT)
                    else:
                        act.wait_ge(x_ready, KD * (n - 1) + k + 1)
                    act.activation(squares[:, k, 0:T], x[:, k, 0:T], ACT.Square).then_inc(squared, 1)
                if n == 0:
                    for v in range(LOOK):
                        split_high(v, v % SLOTS, 512, 32 * (v // SLOTS + 2))
                for k in range(KD):
                    act.wait_ge(hf_step, HF_FULL(n, k))
                    act.activation(h_hi[:, k, 0:T], hf[:, k % 3, 0:T], ACT.Copy).then_inc(h_hi_ready, 1)

            def ffn(f):
                layer, sub, T = FFNS[f]
                w0 = ffn_first[f]

                def drain_up(g, parity):
                    banks = banks_of(parity)
                    for i in range(2):
                        act.wait_ge(tile_done[f], g * 4 + (2 * i + 1))
                        if not (f == 0 and isinstance(g, int) and g == 0):
                            act.wait_ge(u_ready, g * 2 + (KF * f + i - 1))
                        act.activation(uf[:, i, 0:T], ps[:, banks[2 * i], 0:T], ACT.Silu).then_inc(sil_a, 1)
                    for i in range(2):
                        act.wait_ge(uf_ready, g * 2 + (KF * f + i + 1))
                        dst = u_hi[:, bass.ds(g * 2 + i, 1), 0:T] if not isinstance(g, int) else u_hi[:, 2 * g + i:2 * g + i + 1, 0:T]
                        act.activation(dst, uf[:, i:i + 1, 0:T], ACT.Copy).then_inc(u_hi_ready, 1)

                for j in range(4):
                    split_ahead(w0 + j)
                drain_up(0, 0)
                with act.Fori(0, UP_GROUPS // 2) as i:
                    for half in range(2):
                        for j in range(4):
                            split_ahead_in_loop(w0 + 4 + 4 * half, j, 8, i)
                        drain_up(i * 2 + (1 + half), 1 + half)
                wd = w0 + 4 * UP_GROUPS
                for half in range(2):
                    with act.Fori(0, DOWN_PAIRS // 4) as i:
                        for j in range(4):
                            split_ahead_in_loop(wd, j, 4, i)
                    for j in range(DOWN_PAIRS // 4 * 4, DOWN_PAIRS):
                        split_ahead(wd + j)
                    wd += DOWN_PAIRS

            def mix(layer):
                T, nc_, S = MIX_T[layer], N_CHUNKS[layer], MIX_T[layer] // SEQ
                w = mix_first[layer]
                small, units = SMALL[layer], UNITS[layer]
                A, B = prm[:, layer, 0:COLS_A], prm[:, layer, COLS_A:]

                def tile_in(name, i):
                    act.wait_ge(mix_done[layer], tiles_before(layer, name) + i + 1)

                for name, _, _, _, pairs, _ in mix_gemms(layer)[:6]:
                    for j in range(pairs):
                        split_ahead(w)
                        w += 1
                    bank0 = 4 * (GEMM_AT[name] % 2)
                    for i in range(in_tiles(layer, name)):
                        bank = bank0 + i
                        if name in ("k", "q"):
                            col = DA if name == "k" else 0
                            tile_in(name, i)
                            act.activation(qk[:, i, col:col + DA], ps[:, bank, :], ACT.Copy)\
                                .then_inc(drained[layer][name], 1)
                        elif name == "sgv":
                            tile_in(name, i)
                            act.activation(sgv[:, i, :], ps[:, bank, 0:SGW], ACT.Gelu)\
                                .then_inc(drained[layer][name], 1)
                        elif name == "f1" and i >= 2:
                            tile_in(name, i)
                            act.activation(sgu[:, i - 2, 0:T], ps[:, bank, 0:T], ACT.Gelu)\
                                .then_inc(drained[layer][name], 1)
                        elif name in ("f0", "f1"):
                            c = i if name == "f0" else 4 + i
                            tile_in(name, i)
                            act.activation(hy[:, c, 0:T], ps[:, bank, 0:T], ACT.Identity,
                                           bias=B[:, 18 + c:19 + c], scale=B[:, 6 + c:7 + c])\
                                .then_inc(conv_ready[layer], 1)

                def small_in(step):
                    act.wait_ge(small_done[layer], small[step] + 1)
                    return ps[:, 4 + 2 * (small[step] % 2):6 + 2 * (small[step] % 2), :]

                def free(step):
                    return slot_free[layer][small[step] % 2]

                for step in SCHED[layer]:
                    kind = step[0]
                    if kind == "pair":
                        split_ahead(w)
                        w += 1
                    elif kind == "drain":
                        name = step[1]
                        if name.startswith("gate_"):
                            branch, g = "abc".index(name[5]), int(name[6])
                            for i in range(4):
                                tile_in(name, i)
                                if name == "gate_c0":
                                    act.wait_ge(ws_ready[layer], 1)
                                else:
                                    before = f"br_{'abc'[branch]}0" if g else f"br_{'bc'[branch] if branch < 2 else ''}1"
                                    act.wait_ge(drained[layer][before], i + 1)
                                col = 96 + branch * KD + g * 4 + i
                                act.activation(gate[:, i, 0:T], ps[:, i, 0:T], ACT.Sigmoid,
                                               bias=A[:, col:col + 1]).then_inc(drained[layer][name], 1)
                    elif kind == "qk_turn":
                        c, bank = step[1], small_in(step)
                        if c < nc_:
                            act.activation(qT[:, :, c * P:(c + 1) * P], bank[:, 0, :].rearrange("p (h n) -> p h n", h=HEADS),
                                           ACT.Copy)
                        act.activation(kT[:, :, c * P:(c + 1) * P], bank[:, 1, :].rearrange("p (h n) -> p h n", h=HEADS),
                                       ACT.Copy).then_inc(qkT_ready[layer], 1)
                        act.wait_ge(qkT_ready[layer], c + 1)
                        act.sem_inc(free(step), 1)
                    elif kind == "sg_mix":
                        for i in range(2):
                            act.wait_ge(yc_full[layer], i + 1)
                            act.activation(yc_hi[:, i, 0:T], sgu[:, i, 0:T], ACT.Copy).then_inc(yc_hi_ready[layer], 1)
                    elif kind == "scores":
                        u = step[1]
                        qcs, key0, h = units[u]
                        bank = small_in(step)
                        act.wait_ge(max_ready[layer], u + 1)
                        if u == 0:
                            act.wait_ge(yc_ready[layer], 2)
                        n = len(qcs)
                        for i in range(2 * n):
                            c, q = i // n, i % n
                            cols = 512 // n
                            ins = act.activation(e[:, c, q * cols:(q + 1) * cols], bank[:, c, q * cols:(q + 1) * cols],
                                                 ACT.Exp, bias=sm[:, i:i + 1], scale=DH ** -0.5,
                                                 accum_out=sm[:, 4 + i:5 + i])
                        ins.then_inc(exp_ready[layer], 1)
                        act.wait_ge(exp_ready[layer], u + 1)
                        act.sem_inc(free(step), 1)
                    elif kind == "turn":
                        u, bank = step[1], small_in(step)
                        if u:
                            act.wait_ge(small_done[layer], small[("mixv", u - 1)] + 1)
                        act.activation(aT[:, :], bank[:, 0, :], ACT.Copy).then_inc(aT_ready[layer], 1)
                        act.wait_ge(aT_ready[layer], u + 1)
                        act.sem_inc(free(step), 1)
                    elif kind == "mixv":
                        u, bank = step[1], small_in(step)
                        qcs, _, h = units[u]
                        for i, qc in enumerate(qcs):
                            ins = act.activation(o_tok[qc][:, h * DV:(h + 1) * DV], bank[:, 0, i * DV:(i + 1) * DV], ACT.Copy)
                        ins.then_inc(o_ready[layer], 1)
                        act.wait_ge(o_ready[layer], u + 1)
                        act.sem_inc(free(step), 1)
                    elif kind == "h_turn":
                        bank = small_in(step)
                        n = nc_ * HYW
                        act.activation(htok[:, 0:nc_, :].rearrange("p c n -> p (c n)"),
                                       bank.rearrange("p b n -> p (b n)")[:, 0:n], ACT.Copy)\
                            .then_inc(htok_ready[layer], 1)
                        act.wait_ge(htok_ready[layer], step[1] + 1)
                        act.sem_inc(free(step), 1)
                    elif kind == "h_inv" and step[1] == 1 and step[2] == S - 1:
                        act.wait_ge(yb_full[layer], 1)
                        act.activation(yb_hi[:, :, 0:T], hy[:, 0:2, 0:T], ACT.Copy).then_inc(yb_hi_ready[layer], 1)
                    elif kind == "y_turn":
                        c, bank = step[1], small_in(step)
                        for i in range(2):
                            ins = act.activation(ya_hi[:, :, (2 * c + i) * P:(2 * c + i + 1) * P],
                                                 bank[:, i, :].rearrange("p (h n) -> p h n", h=HEADS),
                                                 ACT.Copy, scale=B[:, 28:29])
                        ins.then_inc(ya_hi_ready[layer], 1)

                for k in range(KD):
                    if k == 0:
                        act.wait_ge(mix_done[layer], tiles_before(layer, "gate_a1") + 4)
                    act.wait_ge(drained[layer]["br_a0" if k < 4 else "br_a1"], k % 4 + 1)
                    act.activation(h_hi[:, k, 0:T], merged[:, k, 0:T], ACT.Copy).then_inc(m_hi_ready[layer], 1)
                for g in range(2):
                    for j in range(4):
                        split_ahead(w)
                        w += 1

            for layer in range(DEPTH):
                norm(3 * layer, TOK, sq_h)
                ffn(2 * layer)
                norm(3 * layer + 1, TOK, sq_h)
                mix(layer)
                norm(3 * layer + 2, MIX_T[layer], sq_m)
                ffn(2 * layer + 1)

        @block.tensor
        def _(pe):
            def transpose(dst, src, rows):
                return pe.transpose(dst, src, ident[0:rows, 0:rows])

            pe.wait_ge(const_loaded, 16)
            pe.wait_ge(row_cleared, 1)
            pe.wait_ge(row_loaded, 16 * N_ROWS)
            pe.wait_ge(ones_set, 2)
            transpose(ps[:, MISC, 0:2 * KD], crow[:, :], 2 * KD)
            for layer in range(DEPTH):
                at = 2 * KD + layer * (COLS_A + COLS_B)
                transpose(ps[:, MISC, at:at + COLS_A], prow[0:COLS_A, layer, 0, :], COLS_A)
                ins = transpose(ps[:, MISC, at + COLS_A:at + COLS_A + COLS_B], prow[0:COLS_B, layer, 1, :], COLS_B)
            ins.then_inc(turned, 1)

            for c in range(NT):
                pe.wait_ge(raw_loaded[c], 32)
                if c >= 2:
                    pe.wait_ge(x0_ready, 2 * (c - 1))
                for k in range(KD):
                    bank = 2 * (c % 2) + k // 4
                    ins = transpose(ps[:, bank, (k % 4) * P:(k % 4 + 1) * P], raw[:, c, k * P:(k + 1) * P], P)
                ins.then_inc(xt_done, 1)

            def ada0_group(q):
                if q == 0:
                    pe.wait_ge(sil_ready, 1)
                elif q == 1:
                    pe.wait_ge(prm_ready, 1)
                else:
                    pe.wait_ge(mod_step, q - 1)
                pe.wait_ge(ada0_loaded[q % 3], 16 * (q // 3 + 1))
                for tile in range(4):
                    for k in range(KD):
                        ins = pe.matmul(ps[:, 6 + q % 2, tile * 2:tile * 2 + 2],
                                        ada0[:, q % 3, k * 512 + tile * P:k * 512 + (tile + 1) * P],
                                        sil_c[:, k, :], start=k == 0, stop=k == KD - 1)
                ins.then_inc(ada0_done, 1)

            def filter_step(layer, step):
                v0, a0 = FLT_V * layer, FLT_A * layer
                if step == 0:
                    if layer == 0:
                        pe.wait_ge(flt_loaded, 16 * 6)
                        pe.wait_ge(prm_ready, 1)
                    else:
                        pe.wait_ge(flt_v, FLT_V - 3)
                    ins = pe.matmul(ps[0:FH, 4, 0:SEQ], fw1[:, layer, :], zt[:, :], start=True, stop=True)
                elif step == 1:
                    pe.wait_ge(flt_a, a0 + 1)
                    ins = pe.matmul(ps[0:FH, 5, 0:SEQ], fw2[:, layer, :], f_sin[:, 0, :], start=True, stop=True)
                elif step in (2, 3):
                    c = step - 2
                    pe.wait_ge(flt_a, a0 + 2)
                    if c:
                        pe.wait_ge(flt_v, v0 + 16)
                    for way in range(2):
                        ins = pe.matmul(ps[:, 4 + way, :], f_sin[:, 1, c * P:(c + 1) * P],
                                        fw3[:, layer, way * 512:(way + 1) * 512], start=True, stop=True)
                elif step == 4:
                    pe.wait_ge(flt_a, a0 + 4)
                    for c in range(2):
                        for way in range(2):
                            ins = pe.matmul(ps[:, 4, :], ones[:, :], tmag[:, c, way, :],
                                            start=c + way == 0, stop=c + way == 2)
                else:
                    pe.wait_ge(flt_v, v0 + 21)
                    if layer == 0:
                        pe.wait_ge(x0_ready, 2 * NT)
                    for fc in range(2):
                        for part in range(2):
                            for c in range(2):
                                ins = pe.matmul(ps[:, 2 * fc + part, :], dft_f0[:, c, part, fc * P:(fc + 1) * P],
                                                tmag[:, c, part, :], start=c == 0, stop=c == 1)
                ins.then_inc(flt_pe, 1)

            steps = [(layer, step) for layer in range(DEPTH) for step in range(FLT_P)]
            for q in range(ADA_START):
                ada0_group(q)
                for s in steps[2 * q:2 * q + 2]:
                    filter_step(*s)

            def norm(n, T, squares):
                nt = T // P
                if n > 0:
                    pe.wait_ge(x_ready, KD * (n - 1) + 4)
                else:
                    pe.wait_ge(mod_step, ADA_START)
                for k in range(KD):
                    pe.wait_ge(squared, KD * n + k + 1)
                    for c in range(nt):
                        ins = pe.matmul(ps[:, MISC, c:c + 1], squares[:, k, c * P:(c + 1) * P], ones[:, 0:1],
                                        start=k == 0 and c == 0, stop=k == KD - 1, skip_group_check=True)
                ins.then_inc(sums_done, 1)
                pe.wait_ge(diag_ready, NT * n + nt)
                pe.matmul(ps[:, MISC, 0:T], ones[:, :], diag[:, 0:T], start=True, stop=True).then_inc(rstd_spread, 1)

            def product(out, lhs, rhs, first, last):
                pe.matmul(out, lhs[1], rhs[0], start=first, stop=False)
                pe.matmul(out, lhs[0], rhs[1], start=False, stop=False)
                return pe.matmul(out, lhs[0], rhs[0], start=False, stop=last)

            def feature_pair(w, offsets, banks, moving, k0, T, first, last, done, used=True, before=None):
                slot = w % SLOTS
                for m, off in enumerate(offsets):
                    if before is not None:
                        before(m)
                    for k in range(2):
                        cols = slice(k * 512 + off, k * 512 + off + P)
                        rhs = [v[:, bass.ds(k0 + k, 1), 0:T] if not isinstance(k0, int) else v[:, k0 + k, 0:T]
                               for v in moving]
                        ins = product(ps[:, banks[m], 0:T], (w_hi[:, slot, cols], w_lo[:, slot, cols]), rhs,
                                      first and k == 0, last and k == 1)
                    if last and m < len(offsets) - 1:
                        ins.then_inc(done, 1)
                return ins

            H = (h_hi, h_lo)
            U = (u_hi, u_lo)

            def ffn(f):
                layer, sub, T = FFNS[f]
                w0, n = ffn_first[f], 3 * (f // 2) + 2 * (f % 2)
                uf0 = KF * f

                def fold(G):
                    pe.wait_ge(ada_step, G * 16 + 16)
                    if not isinstance(G, int) or G > 0:
                        pe.wait_ge(ada_taken, G)
                    for tile in range(4):
                        for s in range(2):
                            ins = pe.matmul(ps[:, MISC, tile * 2 + s:tile * 2 + s + 1],
                                            ada_acc[:, s, tile * P:(tile + 1) * P], ones[:, 0:1],
                                            start=True, stop=True)
                    ins.then_inc(ada_folded, 1)

                def up_group(g, parity, w_at, g_in_loop):
                    banks = banks_of(parity)

                    def banks_drained(m):
                        if m == 3 and not (isinstance(g, int) and g == 0):
                            pe.wait_ge(uf_ready, g * 2 + uf0)

                    for j in range(4):
                        pe.wait_ge(lo_ready, g * 4 + (w0 + j + 1))
                        if isinstance(g, int) and g == 0:
                            pe.wait_ge(h_ready, KD * n + 2 * j + 2)
                        ins = feature_pair(w_at + j, up_tiles(), banks, H, 2 * j, T, j == 0, j == 3, tile_done[f],
                                           before=banks_drained if j == 0 else None)
                        if j == 3:
                            ins.then_inc(tile_done[f], 1)
                            pe.wait_ge(tile_done[f], g * 4 + 4)
                            pe.sem_inc(pair_used, 1)
                        else:
                            ins.then_inc(pair_used, 1)

                groups, G0 = ADA_FFN_GROUPS[f], ADA_FFN_FIRST[f]
                up_group(0, 0, w0, 0)
                loops = (groups - 1) // 2 if groups else 0
                if loops:
                    with pe.Fori(0, loops) as i:
                        for half in range(2):
                            fold(i * 2 + (G0 + half))
                            up_group(i * 2 + (1 + half), 1 + half, w0 + 4 + 4 * half, i)
                if groups:
                    fold(G0 + groups - 1)
                if loops < UP_GROUPS // 2:
                    with pe.Fori(loops, UP_GROUPS // 2) as i:
                        for half in range(2):
                            up_group(i * 2 + (1 + half), 1 + half, w0 + 4 + 4 * half, i)

                wd = w0 + 4 * UP_GROUPS
                for half in range(2):
                    banks = banks_of(UP_GROUPS + half)

                    def banks_drained(m):
                        if half == 0:
                            pe.wait_ge(uf_ready, uf0 + KF if m == 3 else uf0 + KF - 2)
                        elif m == 3:
                            pe.wait_ge(x_ready, KD * n + 4)
                        else:
                            pe.wait_ge(uf_ready, uf0 + KF)

                    def down_pair(w, k0, w_value, u_value, first, last):
                        pe.wait_ge(lo_ready, w_value)
                        if half == 0:
                            pe.wait_ge(u_ready, u_value)
                        ins = feature_pair(w, (0, P, 2 * P, 3 * P), banks, U, k0, T, first, last, tile_done[f],
                                           before=banks_drained if first else None)
                        if last:
                            ins.then_inc(tile_done[f], 1)
                            pe.wait_ge(tile_done[f], 4 * (UP_GROUPS + half + 1))
                            pe.sem_inc(pair_used, 1)
                        else:
                            ins.then_inc(pair_used, 1)

                    down_pair(wd, 0, wd + 1, uf0 + 2, True, False)
                    with pe.Fori(0, 2) as i:
                        for j in range(1, 5):
                            down_pair(wd + j, i * 8 + 2 * j, i * 4 + (wd + j + 1), i * 8 + (uf0 + 2 * j + 2), False, False)
                    for j in range(9, DOWN_PAIRS):
                        down_pair(wd + j, 2 * j, wd + j + 1, uf0 + 2 * j + 2, False, j == DOWN_PAIRS - 1)
                    wd += DOWN_PAIRS

            def mix(layer):
                T, nc_, S = MIX_T[layer], N_CHUNKS[layer], MIX_T[layer] // SEQ
                w = mix_first[layer]
                small = SMALL[layer]
                n = 3 * layer + 1
                done = mix_done[layer]
                gemms = {g[0]: g for g in mix_gemms(layer)}

                def end_tile(name, i, ins, last_pair):
                    ins.then_inc(done, 1)
                    if last_pair and i == in_tiles(layer, name) - 1:
                        pe.wait_ge(done, tiles_before(layer, name) + in_tiles(layer, name))
                        pe.sem_inc(pair_used, 1)

                def token_pair(name, j, w):
                    cols = gemms[name][5]
                    bank0 = 4 * (GEMM_AT[name] % 2)
                    tiles = in_tiles(layer, name)
                    for i in range(tiles):
                        if j == 0 and GEMM_AT[name] >= 2:
                            before = mix_gemms(layer)[GEMM_AT[name] - 2][0]
                            if i < in_tiles(layer, before):
                                pe.wait_ge(drained[layer][before], i + 1)
                        for k in range(2):
                            lhs = [v[:, 2 * j + k, i * P:(i + 1) * P] for v in H]
                            rhs = [v[:, w % SLOTS, k * 512:k * 512 + cols] for v in (w_hi, w_lo)]
                            ins = product(ps[:, bank0 + i, 0:cols], lhs, rhs, j == 0 and k == 0, j == 3 and k == 1)
                        if j == 3:
                            end_tile(name, i, ins, True)
                    if j < 3:
                        ins.then_inc(pair_used, 1)

                def mix_pair(name, j, w, banks, moving, before):
                    last = j == gemms[name][4] - 1
                    ins = feature_pair(w, (0, P, 2 * P, 3 * P), banks, moving, 2 * j, T, j == 0, last, done,
                                       before=before if j == 0 else None)
                    if last:
                        end_tile(name, 3, ins, True)
                    else:
                        ins.then_inc(pair_used, 1)

                for name in ("k", "q", "v", "sgv", "f0", "f1"):
                    for j in range(4):
                        pe.wait_ge(lo_ready, w + 1)
                        if name == "k":
                            pe.wait_ge(h_ready, KD * n + 2 * j + 2)
                        if name in ("f0", "f1"):
                            before = "v" if name == "f0" else "sgv"
                            mix_pair(name, j, w, tuple(range(4 * (name == "f1"), 4 * (name == "f1") + 4)), H,
                                     lambda m: pe.wait_ge(drained[layer][before], min(m + 1, in_tiles(layer, before))))
                        else:
                            token_pair(name, j, w)
                        w += 1

                def small_at(step):
                    n = small[step]
                    if n < 2:
                        pe.wait_ge(drained[layer]["f1"], 4)
                    else:
                        pe.wait_ge(slot_free[layer][n % 2], n // 2)
                    return ps[:, 4 + 2 * (n % 2):6 + 2 * (n % 2), :]

                units = UNITS[layer]
                for step in SCHED[layer]:
                    kind = step[0]
                    if kind == "pair":
                        name, j = step[1:]
                        pe.wait_ge(lo_ready, w + 1)
                        if name.startswith("gate_"):
                            at = GEMM_AT[name]
                            before = mix_gemms(layer)[at - 1][0] if name != "gate_c0" else "f0"
                            mix_pair(name, j, w, (0, 1, 2, 3), H,
                                     lambda m: pe.wait_ge(drained[layer][before], m + 1))
                        else:
                            branch = name[3]
                            before = "gate_" + name[3:]
                            if j == 0:
                                pe.wait_ge({"a": ya_ready, "b": yb_ready, "c": yc_ready}[branch][layer],
                                           {"a": S, "b": 1, "c": 2}[branch])
                            mix_pair(name, j, w, (0, 1, 2, 3),
                                     {"a": (ya_hi, ya_lo), "b": (yb_hi, yb_lo), "c": (yc_hi, yc_lo)}[branch],
                                     lambda m: pe.wait_ge(drained[layer][before], m + 1))
                        w += 1
                        continue
                    if kind == "drain":
                        continue
                    bank = small_at(step)
                    if kind == "ws_turn":
                        pe.wait_ge(mixc_loaded[layer], 16 * 9)
                        for g in range(4):
                            ins = transpose(bank[:, 0, g * P:(g + 1) * P], ws[:, g, :], P)
                    elif kind == "qk_turn":
                        c = step[1]
                        pe.wait_ge(qk_normed[layer], c + 1)
                        for h in range(HEADS):
                            if c < nc_:
                                transpose(bank[:, 0, h * P:(h + 1) * P], qk[:, c, h * P:(h + 1) * P], P)
                            ins = transpose(bank[:, 1, h * P:(h + 1) * P], qk[:, c, DA + h * P:DA + (h + 1) * P], P)
                    elif kind == "sg_mix":
                        pe.wait_ge(ln_done[layer], nc_)
                        pe.wait_ge(ws_ready[layer], 1)
                        for c in range(nc_):
                            for g in range(4):
                                ins = pe.matmul(bank[64 * (g % 2):64 * (g % 2) + 64, g // 2, c * P:(c + 1) * P],
                                                sgv[:, c, g * 64:(g + 1) * 64], wsT[:, g, :], start=True, stop=True)
                    elif kind == "scores":
                        qcs, key0, h = units[step[1]]
                        pe.wait_ge(qkT_ready[layer], 4)
                        cols = 512 // len(qcs)
                        for c in range(2):
                            rows = slice(c * DH, (c + 1) * DH)
                            for i, qc in enumerate(qcs):
                                ins = pe.matmul(bank[:, c, i * cols:(i + 1) * cols], qT[rows, h, qc * P:(qc + 1) * P],
                                                kT[rows, h, key0 * P:key0 * P + cols], start=True, stop=True)
                    elif kind == "turn":
                        pe.wait_ge(a_ready[layer], step[1] + 1)
                        for i in range(4):
                            ins = transpose(bank[:, 0, i * P:(i + 1) * P], e[:, 0, i * P:(i + 1) * P], P)
                    elif kind == "mixv":
                        qcs, key0, h = units[step[1]]
                        pe.wait_ge(aT_ready[layer], step[1] + 1)
                        pe.wait_ge(drained[layer]["v"], 4)
                        n = 4 // len(qcs)
                        for i in range(len(qcs)):
                            for k in range(n):
                                ins = pe.matmul(bank[:, 0, i * DV:(i + 1) * DV], aT[:, (i * n + k) * P:(i * n + k + 1) * P],
                                                vtok[:, key0 + k, h * DV:(h + 1) * DV], start=k == 0, stop=k == n - 1)
                    elif kind == "h_turn":
                        order = step[1]
                        if order == 0:
                            pe.wait_ge(drained[layer]["f0"], 2)
                        else:
                            pe.wait_ge(z_ready[layer], S)
                        for c in range(nc_):
                            for i in range(2):
                                ins = transpose(bank[:, c // 2, (c % 2) * HYW + i * P:(c % 2) * HYW + (i + 1) * P],
                                                hy[:, 2 * order + i, c * P:(c + 1) * P], P)
                    elif kind == "h_fwd":
                        _, order, s = step
                        pe.wait_ge(htok_ready[layer], order + 1)
                        pe.wait_ge(dft_loaded[layer], 16 * 5)
                        for part in range(2):
                            for fc in range(2):
                                for c in range(2):
                                    ins = pe.matmul(bank[:, part, fc * HYW:(fc + 1) * HYW],
                                                    dft[:, c, 0, part, fc * P:(fc + 1) * P], htok[:, 2 * s + c, :],
                                                    start=c == 0, stop=c == 1)
                    elif kind == "h_inv":
                        _, order, s = step
                        pe.wait_ge(hprod_ready[layer], order * S + s + 1)
                        for i in range(2):
                            for fc in range(2):
                                for part in range(2):
                                    ins = pe.matmul(bank[:, 0, i * SEQ:(i + 1) * SEQ],
                                                    hprod[:, fc, part, i * P:(i + 1) * P], dft[:, fc, 1, part, :],
                                                    start=fc + part == 0, stop=fc + part == 2)
                    elif kind == "y_turn":
                        c = step[1]
                        pe.wait_ge(o_normed[layer], nc_)
                        for i in range(2):
                            for h in range(HEADS):
                                ins = transpose(bank[:, i, h * P:(h + 1) * P], o_tok[2 * c + i][:, h * DV:(h + 1) * DV], P)
                    ins.then_inc(small_done[layer], 1)

                for g in range(2):
                    for j in range(4):
                        pe.wait_ge(lo_ready, w + 1)
                        if g == 0:
                            pe.wait_ge(m_ready[layer], 2 * j + 2)
                        if j == 0 and g == 0:
                            for b in range(2):
                                pe.wait_ge(slot_free[layer][b], (len(small) + 1 - b) // 2)

                        def before(m):
                            if g == 1:
                                pe.wait_ge(drained[layer]["br_a1"], m + 1)
                        mix_pair(f"o{g}", j, w, tuple(range(4 - 4 * g, 8 - 4 * g)), H, before)
                        w += 1

            norm(0, TOK, sq_h)
            ffn(0)
            norm(1, TOK, sq_h)
            mix(0)
            norm(2, TOK, sq_m)
            ffn(1)
            norm(3, TOK, sq_h)
            ffn(2)
            norm(4, TOK, sq_h)
            mix(1)
            norm(5, SEQ, sq_m)
            ffn(3)
            for c in range(2):
                pe.wait_ge(x_ready, KD * 6)
                for k in range(KD):
                    ins = transpose(ps[:, (4 if c == 0 else 0) + k // 4, (k % 4) * P:(k % 4 + 1) * P],
                                    x[:, k, c * P:(c + 1) * P], P)
                ins.then_inc(out_turned, 1)

        @block.vector
        def _(dve):
            chain = Chain(dve, v_step)

            def link(ins):
                chain.step(ins)
                chain.after()

            dve.memset(ms[:, :], 1.0).then_inc(v_step, 1)
            chain.n += 1
            dve.wait_ge(sil_ready, 1)
            link(dve.tensor_copy(prm[:, :, :].rearrange("p l c -> p (l c)"),
                                 ps[:, MISC, 2 * KD:2 * KD + DEPTH * (COLS_A + COLS_B)]))
            for layer in range(DEPTH):
                col = prm[:, layer, COLS_A + 28:COLS_A + 29]
                ins = dve.tensor_scalar(col, col, 1.0 - lam_init(layer), None, ALU.mult)
                link(ins) if layer == 0 else ins.then_inc(prm_ready, 1)
            dve.wait_ge(prm_ready, 1)

            for c in range(NT):
                dve.wait_ge(xt_done, c + 1)
                for i in range(2):
                    dve.tensor_copy(x[:, 4 * i:4 * i + 4, c * P:(c + 1) * P],
                                    ps[:, 2 * (c % 2) + i, :].rearrange("p (k n) -> p k n", k=4)).then_inc(x0_ready, 1)

            dve.wait_ge(lv_loaded, 16 * DEPTH)
            for layer in range(DEPTH):
                pairs = lv[:, layer, :, :].rearrange("p (i j) n -> p i j n", j=2)
                dve.tensor_tensor(pairs[:, :, 0, :], pairs[:, :, 0, :], pairs[:, :, 1, :], ALU.mult).then_inc(lam_v, 1)
                dve.wait_ge(lam_v, 2 * layer + 1)
                dve.tensor_reduce(lsum[:, 2 * layer:2 * layer + 2], pairs[:, :, 0, :], AX.X, ALU.add).then_inc(lam_v, 1)
            dve.wait_ge(lam_a, 1)
            for layer in range(DEPTH):
                dve.scalar_tensor_tensor(lam[:, layer:layer + 1], lsum[:, 2 * layer + 1:2 * layer + 2],
                                         -lam_init(layer), lsum[:, 2 * layer:2 * layer + 1],
                                         ALU.add, ALU.subtract).then_inc(v_step, 1)
                chain.n += 1

            def mod_out(q, src):
                layer, g = q // ADA_GROUPS, q % ADA_GROUPS
                return dve.tensor_tensor(mod[:, layer, 4 * g:4 * g + 4, :], src.rearrange("p (t s) -> p t s", s=2),
                                         prm[:, layer, 4 * g:4 * g + 4].unsqueeze(2).broadcast_to([P, 4, 2]), ALU.add)

            MAGIC = 1.5 * 2.0 ** 23
            TURN = (6.28125, 1.9340515136718750e-3, 2.0 * math.pi - 6.28125 - 1.9340515136718750e-3)
            SIN_MAX = 3.1415925

            def filter_step(layer, step):
                v0, p0 = FLT_V * layer, FLT_P * layer
                Bc = prm[:, layer, COLS_A:]
                count = [v0 + (0, 7, 14, 16, 18, 21)[step]]

                def flt(ins, wait=True):
                    count[0] += 1
                    ins.then_inc(flt_v, 1)
                    if wait:
                        dve.wait_ge(flt_v, count[0])

                dve.wait_ge(flt_pe, p0 + step + 1)
                if step < 2:
                    if step == 0 and layer:
                        dve.wait_ge(flt_a, FLT_A * layer)
                    flt(dve.tensor_scalar(f_arg[:, :], ps[0:FH, 4 + step, 0:SEQ], Bc[0:FH, 29 + step:30 + step],
                                          Bc[0:FH, 31:32], ALU.add, ALU.mult))
                    flt(dve.tensor_scalar(f_turns[:, :], f_arg[:, :], 0.5 / math.pi, MAGIC, ALU.mult, ALU.add))
                    flt(dve.tensor_scalar(f_turns[:, :], f_turns[:, :], -MAGIC, None, ALU.add))
                    for part in TURN:
                        flt(dve.scalar_tensor_tensor(f_arg[:, :], f_turns[:, :], -part, f_arg[:, :], ALU.mult, ALU.add))
                    flt(dve.tensor_scalar(f_arg[:, :], f_arg[:, :], SIN_MAX, -SIN_MAX, ALU.min, ALU.max))
                elif step < 4:
                    c = step - 2
                    if layer and c == 0:
                        dve.wait_ge(spec_stored, 16)
                    for way in range(2):
                        flt(dve.tensor_tensor(taps[:, c, way, :], ps[:, 4 + way, :], decay[:, c, way, :], ALU.mult),
                            wait=way == 1)
                elif step == 4:
                    flt(dve.reciprocal(inv_l1[:, :], ps[:, 4, :]))
                    flt(dve.tensor_tensor(tmag[:, :, 0, :], taps[:, :, 0, :], taps[:, :, 1, :], ALU.add))
                    flt(dve.tensor_tensor(tmag[:, :, 1, :], taps[:, :, 1, :], taps[:, :, 0, :], ALU.subtract))
                else:
                    flt(dve.tensor_tensor(spec0[:, :, :, :].rearrange("p a b n -> p (a b) n"), ps[:, 0:4, :],
                                          inv_l1[:, :].unsqueeze(1).broadcast_to([P, 4, 512]), ALU.mult))

            steps = [(layer, step) for layer in range(DEPTH) for step in range(FLT_P)]
            for q in range(ADA_START):
                dve.wait_ge(ada0_done, q + 1)
                mod_out(q, ps[:, 6 + q % 2, 0:8]).then_inc(mod_step, 1)
                for s in steps[2 * q:2 * q + 2]:
                    filter_step(*s)

            def modulation(n):
                layer, sub = n // 3, n % 3
                first = 3 * sub * KD
                scale = mod[:, layer, first + KD:first + 2 * KD, :]
                chain.step(dve.scalar_tensor_tensor(
                    mod_a[:, n, :, :], scale, 1.0,
                    prm[:, layer, 72 + sub * KD:72 + (sub + 1) * KD].unsqueeze(2).broadcast_to([P, KD, 2]),
                    ALU.add, ALU.mult))
                chain.step(dve.tensor_scalar(mod_g[:, n, :, :], mod[:, layer, first + 2 * KD:first + 3 * KD, :],
                                             0.5 if sub != 1 else 1.0, None, ALU.mult))
                chain.after()

            def norm(n, T, request):
                nt, S = T // P, T // SEQ
                layer, sub = n // 3, n % 3
                if n == 0:
                    dve.wait_ge(mod_step, ADA_START)
                else:
                    dve.wait_ge(ada_taken, sum(ADA_FFN_GROUPS[:(2 * n + 1) // 3]))
                modulation(n)
                dve.wait_ge(sums_done, n + 1)
                dve.tensor_scalar(ms[:, 0:nt], ps[:, MISC, 0:nt], 1.0 / D, EPS, ALU.mult, ALU.add).then_inc(ms_ready, 1)
                dve.wait_ge(rstd_ready, request + 1)
                for c in range(nt):
                    dve.tensor_scalar(diag[:, c * P:(c + 1) * P], ident[:, :], rstd[:, c:c + 1], None, ALU.mult)\
                        .then_inc(diag_ready, 1)
                dve.wait_ge(rstd_spread, n + 1)

                def low(k):
                    dve.wait_ge(h_hi_ready, KD * n + k + 1)
                    dve.tensor_tensor(h_lo[:, k, 0:T], hf[:, k % 3, 0:T], h_hi[:, k, 0:T].bitcast(F32),
                                      ALU.subtract).then_inc(h_ready, 1)

                for k in range(KD):
                    if k >= 3:
                        dve.wait_ge(h_ready, KD * n + k - 2)
                    dve.tensor_tensor(hf[:, k % 3, 0:T], x[:, k, 0:T], ps[:, MISC, 0:T], ALU.mult).then_inc(hf_step, 1)
                    dve.wait_ge(hf_step, HF_FULL(n, k) - S)
                    for s in range(S):
                        part = hf[:, k % 3, s * SEQ:(s + 1) * SEQ]
                        dve.tensor_scalar(part, part, mod_a[:, n, k, s:s + 1],
                                          mod[:, layer, 3 * sub * KD + k, s:s + 1], ALU.mult, ALU.add).then_inc(hf_step, 1)
                    if k:
                        low(k - 1)
                low(KD - 1)

            def split_low(slot, cols, hi_value):
                dve.wait_ge(hi_ready, hi_value)
                view = [v.rearrange("p (k n) -> p k n", k=2)[:, :, 0:cols]
                        for v in (w_lo[:, slot, :], raw[:, slot, :], w_hi[:, slot, :].bitcast(F32))]
                dve.tensor_tensor(view[0], view[1], view[2], ALU.subtract).then_inc(lo_ready, 1)

            def split_ahead(w):
                v = w + LOOK
                if v < N_PAIRS:
                    split_low(v % SLOTS, pair_cols(v), v + 1)

            def ffn(f):
                layer, sub, T = FFNS[f]
                w0, n, S = ffn_first[f], 3 * (f // 2) + 2 * (f % 2), FFNS[f][2] // SEQ
                uf0 = KF * f

                def ada_unit(G, j):
                    dve.wait_ge(ada_loaded[j % 2], G * 32 + 16 * (j // 2 + 1))
                    if j == 0 and not (isinstance(G, int) and G == 0):
                        dve.wait_ge(ada_folded, G)
                    for k in range(2):
                        for s in range(2):
                            src = ada_raw[:, j % 2, k * 512:(k + 1) * 512]
                            scalar = sil_c[:, 2 * j + k, s:s + 1]
                            o = 4 * j + 2 * k + s
                            if o < 2:
                                ins = dve.tensor_scalar(ada_acc[:, s, :], src, scalar, None, ALU.mult)
                            else:
                                dve.wait_ge(ada_step, G * 16 + (o - 1))
                                ins = dve.scalar_tensor_tensor(ada_acc[:, s, :], src, scalar, ada_acc[:, s, :],
                                                               ALU.mult, ALU.add)
                            ins.then_inc(ada_step, 1)

                def ada_take(G, q):
                    dve.wait_ge(ada_folded, G + 1)
                    la = (ADA_START + ADA_FFN_FIRST[f]) // ADA_GROUPS
                    at = bass.ds(q * 4, 4) if not isinstance(q, int) else slice(4 * q, 4 * q + 4)
                    dve.tensor_tensor(mod[:, la, at, :],
                                      ps[:, MISC, 0:8].rearrange("p (t s) -> p t s", s=2),
                                      prm[:, la, at].unsqueeze(2).broadcast_to([P, 4, 2]), ALU.add).then_inc(ada_taken, 1)

                def drain_up(g, parity):
                    banks = banks_of(parity)
                    for i in range(2):
                        dve.wait_ge(tile_done[f], g * 4 + (2 * i + 2))
                        dve.wait_ge(sil_a, g * 2 + (uf0 + i + 1))
                        dve.tensor_tensor(uf[:, i, 0:T], uf[:, i, 0:T], ps[:, banks[2 * i + 1], 0:T], ALU.mult)\
                            .then_inc(uf_ready, 1)
                    for i in range(2):
                        dve.wait_ge(u_hi_ready, g * 2 + (uf0 + i + 1))
                        at = slice(2 * g + i, 2 * g + i + 1) if isinstance(g, int) else bass.ds(g * 2 + i, 1)
                        dve.tensor_tensor(u_lo[:, at, 0:T], uf[:, i:i + 1, 0:T], u_hi[:, at, 0:T].bitcast(F32),
                                          ALU.subtract).then_inc(u_ready, 1)

                groups, G0 = ADA_FFN_GROUPS[f], ADA_FFN_FIRST[f]
                q0 = (ADA_START + G0) % ADA_GROUPS
                for j in range(4):
                    split_ahead(w0 + j)
                    if groups:
                        ada_unit(G0, j)
                drain_up(0, 0)
                loops = (groups - 1) // 2 if groups else 0

                def split_in_loop(w, turns, i):
                    v = w + LOOK
                    split_low(v % SLOTS, 512, i * turns + (v + 1))

                if loops:
                    with dve.Fori(0, loops) as i:
                        for half in range(2):
                            ada_take(i * 2 + (G0 + half), i * 2 + (q0 + half))
                            for j in range(4):
                                split_in_loop(w0 + 4 + 4 * half + j, 8, i)
                                ada_unit(i * 2 + (G0 + 1 + half), j)
                            drain_up(i * 2 + (1 + half), 1 + half)
                if groups:
                    ada_take(G0 + groups - 1, q0 + groups - 1)
                if loops < UP_GROUPS // 2:
                    with dve.Fori(loops, UP_GROUPS // 2) as i:
                        for half in range(2):
                            for j in range(4):
                                split_in_loop(w0 + 4 + 4 * half + j, 8, i)
                            drain_up(i * 2 + (1 + half), 1 + half)

                wd = w0 + 4 * UP_GROUPS
                for half in range(2):
                    with dve.Fori(0, DOWN_PAIRS // 4) as i:
                        for j in range(4):
                            split_in_loop(wd + j, 4, i)
                    for j in range(DOWN_PAIRS // 4 * 4, DOWN_PAIRS):
                        split_ahead(wd + j)
                    wd += DOWN_PAIRS
                    banks = banks_of(UP_GROUPS + half)
                    for m in range(4):
                        dve.wait_ge(tile_done[f], 4 * (UP_GROUPS + half) + m + 1)
                        residual(n, 4 * half + m, banks[m], S)

            def residual(n, k, bank, S):
                for s in range(S):
                    part = x[:, k, s * SEQ:(s + 1) * SEQ]
                    ins = dve.scalar_tensor_tensor(part, ps[:, bank, s * SEQ:(s + 1) * SEQ], mod_g[:, n, k, s:s + 1],
                                                   part, ALU.mult, ALU.add)
                ins.then_inc(x_ready, 1)

            def mix(layer):
                T, nc_, S = MIX_T[layer], N_CHUNKS[layer], MIX_T[layer] // SEQ
                w = mix_first[layer]
                small, units = SMALL[layer], UNITS[layer]
                Bc = prm[:, layer, COLS_A:]
                drain = drained[layer]

                def tile_in(name, i):
                    dve.wait_ge(mix_done[layer], tiles_before(layer, name) + i + 1)

                def head_squares(c):
                    first = 0 if c < nc_ else 8
                    if c == 0:
                        dve.wait_ge(drain["k"], 4)
                        dve.wait_ge(drain["q"], nc_)
                        dve.wait_ge(mixc_loaded[layer], 16 * 9)
                    else:
                        chain.after()
                    src = qk[:, c, first * DH:]
                    link(dve.tensor_tensor(tmp[:, 0:(16 - first) * DH], src, src, ALU.mult))
                    chain.step(dve.tensor_reduce(ms[:, 16 * c + first:16 * c + 16],
                                                 tmp[:, 0:(16 - first) * DH].rearrange("p (h n) -> p h n", n=DH),
                                                 AX.X, ALU.add))
                    if c == NT - 1:
                        chain.after()
                        dve.tensor_scalar(ms[:, :], ms[:, :], 1.0 / DH, EPS, ALU.mult, ALU.add).then_inc(ms_ready, 1)

                def head_norm(c):
                    first = 0 if c < nc_ else 8
                    if c == 0:
                        dve.wait_ge(rstd_ready, power_request(layer, "qk") + 1)
                    part = qk[:, c, first * DH:].rearrange("p (h n) -> p h n", n=DH)
                    link(dve.tensor_tensor(part, part, rstd[:, 16 * c + first:16 * c + 16].unsqueeze(2)
                                           .broadcast_to([P, 16 - first, DH]), ALU.mult))
                    both = qk[:, c, first * DH:].rearrange("p (s h n) -> p s h n", n=DH, h=8)
                    gain = qk_gain[:, first // 8:, :].unsqueeze(2).broadcast_to([P, 2 - first // 8, 8, DH])
                    ins = dve.tensor_tensor(both, both, gain, ALU.mult)
                    if c >= 2:
                        ins.then_inc(qk_normed[layer], 1)
                        return
                    link(ins)
                    if c:
                        dve.wait_ge(qk_normed[layer], c)
                    pairs = qk[:, c, :].rearrange("p (g a s n) -> p g a s n", a=2, s=2, n=16)
                    cos, sin = [rope[:, c, i, :].rearrange("p (a n) -> p a n", a=2).unsqueeze(1)
                                .broadcast_to([P, 16, 2, 16]) for i in range(2)]
                    t1, t2 = [tmp[:, i * 512:(i + 1) * 512].rearrange("p (g a n) -> p g a n", g=16, a=2) for i in range(2)]
                    x1, x2 = pairs[:, :, :, 0, :], pairs[:, :, :, 1, :]
                    chain.step(dve.tensor_tensor(t1, x1, sin, ALU.mult))
                    chain.step(dve.tensor_tensor(t2, x2, sin, ALU.mult))
                    chain.after()
                    chain.step(dve.tensor_tensor(x1, x1, cos, ALU.mult))
                    chain.step(dve.tensor_tensor(x2, x2, cos, ALU.mult))
                    chain.after()
                    link(dve.tensor_tensor(x1, x1, t2, ALU.subtract))
                    dve.tensor_tensor(x2, x2, t1, ALU.add).then_inc(qk_normed[layer], 1)

                def ln_stats(c):
                    if c == 0:
                        dve.wait_ge(drain["sgv"], nc_)
                    link(dve.bn_stats(stats[:, c, 0:6], sgv[:, c, :]))
                    chain.step(dve.bn_aggr(stats[:, c, 6:8], stats[:, c, 0:6]))
                    if c == nc_ - 1:
                        chain.after()
                        dve.tensor_scalar(ms[:, 0:nc_], stats[:, 0:nc_, 7], EPS, None, ALU.add).then_inc(ms_ready, 1)

                def ln_apply(c):
                    if c == 0:
                        dve.wait_ge(rstd_ready, power_request(layer, "ln") + 1)
                    part = sgv[:, c, :]
                    link(dve.tensor_scalar(part, part, stats[:, c, 6:7], rstd[:, c:c + 1], ALU.subtract, ALU.mult))
                    link(dve.tensor_tensor(part, part, ln_g[:, :], ALU.mult))
                    dve.tensor_tensor(part, part, ln_b[:, :], ALU.add).then_inc(ln_done[layer], 1)

                extras = {("sgv", j): (head_squares, j) for j in range(4)}
                extras |= {("f0", j): (head_norm, j) for j in range(4)}
                extras |= {("f1", j): (ln_stats, j) for j in range(nc_)}
                for name in ("k", "q", "v", "sgv", "f0", "f1"):
                    for j in range(4):
                        split_ahead(w)
                        w += 1
                        if (name, j) in extras:
                            what, c = extras[name, j]
                            what(c)
                    bank0 = 4 * (GEMM_AT[name] % 2)
                    if name == "v":
                        for i in range(4):
                            tile_in(name, i)
                            dve.tensor_copy(vtok[:, i, :], ps[:, bank0 + i, :]).then_inc(drain[name], 1)
                    if name in ("f0", "f1"):
                        for i in range(4 if name == "f0" else 2):
                            c = i if name == "f0" else 4 + i
                            dve.wait_ge(conv_ready[layer], c + 1)
                            for tap, to, of in ((0, slice(1, SEQ), slice(0, SEQ - 1)), (2, slice(0, SEQ - 1), slice(1, SEQ))):
                                for s in range(S):
                                    dst = hy[:, c, s * SEQ + to.start:s * SEQ + to.stop]
                                    src = ps[:, bank0 + i, s * SEQ + of.start:s * SEQ + of.stop]
                                    ins = dve.scalar_tensor_tensor(dst, src, Bc[:, 6 * tap + c:6 * tap + c + 1], dst,
                                                                   ALU.mult, ALU.add)
                                    if tap == 0 or s < S - 1:
                                        chain.step(ins)
                                    if tap == 0 and s == S - 1:
                                        chain.after()
                            ins.then_inc(drain[name], 1)
                for c in range(nc_):
                    ln_apply(c)

                def small_in(step):
                    dve.wait_ge(small_done[layer], small[step] + 1)
                    return ps[:, 4 + 2 * (small[step] % 2):6 + 2 * (small[step] % 2), :]

                def free(step):
                    return slot_free[layer][small[step] % 2]

                for step in SCHED[layer]:
                    kind = step[0]
                    if kind == "pair":
                        split_ahead(w)
                        w += 1
                    elif kind == "drain" and step[1].startswith("br_"):
                        name = step[1]
                        branch, g = name[3], int(name[4])
                        for i in range(4):
                            dve.wait_ge(drain["gate_" + name[3:]], i + 1)
                            tile_in(name, i)
                            part = merged[:, 4 * g + i, 0:T]
                            if branch == "c":
                                dve.tensor_tensor(part, gate[:, i, 0:T], ps[:, i, 0:T], ALU.mult).then_inc(drain[name], 1)
                            else:
                                link(dve.tensor_tensor(gate[:, i, 0:T], gate[:, i, 0:T], ps[:, i, 0:T], ALU.mult))
                                dve.tensor_tensor(part, part, gate[:, i, 0:T], ALU.add).then_inc(drain[name], 1)
                    elif kind == "ws_turn":
                        bank = small_in(step)
                        dve.tensor_copy(wsT[:, :, :].rearrange("p g n -> p (g n)"), bank[:, 0, :]).then_inc(ws_ready[layer], 1)
                        dve.wait_ge(ws_ready[layer], 1)
                        dve.sem_inc(free(step), 1)
                    elif kind == "sg_mix":
                        bank = small_in(step)
                        for i in range(2):
                            part = tmp[:, i * 512:i * 512 + T]
                            ins = dve.tensor_tensor(part.rearrange("p (c n) -> p c n", n=P),
                                                    bank[:, i, 0:T].rearrange("p (c n) -> p c n", n=P),
                                                    sgb[:, i, :].unsqueeze(1).broadcast_to([P, nc_, P]), ALU.add)
                            link(ins)
                            if i == 0:
                                dve.wait_ge(drain["f1"], 4)
                            dve.tensor_tensor(sgu[:, i, 0:T], part, sgu[:, i, 0:T], ALU.mult).then_inc(yc_full[layer], 1)
                        dve.sem_inc(free(step), 1)
                        for i in range(2):
                            dve.wait_ge(yc_hi_ready[layer], i + 1)
                            dve.tensor_tensor(yc_lo[:, i, 0:T], sgu[:, i, 0:T], yc_hi[:, i, 0:T].bitcast(F32),
                                              ALU.subtract).then_inc(yc_ready[layer], 1)
                    elif kind == "scores":
                        u, bank = step[1], small_in(step)
                        n = 2 * len(units[u][0])
                        link(dve.tensor_reduce(sm[:, 0:n], bank.rearrange("p b (i n) -> p (b i) n", i=n // 2),
                                               AX.X, ALU.max))
                        dve.tensor_scalar(sm[:, 0:n], sm[:, 0:n], -DH ** -0.5, None, ALU.mult).then_inc(max_ready[layer], 1)
                    elif kind == "turn":
                        u = step[1]
                        m = len(units[u][0])
                        dve.wait_ge(exp_ready[layer], u + 1)
                        link(dve.reciprocal(sm[:, 8:8 + 2 * m], sm[:, 4:4 + 2 * m]))
                        link(dve.tensor_scalar(sm[:, 8 + m:8 + 2 * m], sm[:, 8 + m:8 + 2 * m], lam[:, layer:layer + 1],
                                               None, ALU.mult))
                        cols = 512 // m
                        for i in range(m):
                            at = slice(i * cols, (i + 1) * cols)
                            link(dve.tensor_scalar(e[:, 1, at], e[:, 1, at], sm[:, 8 + m + i:9 + m + i], None, ALU.mult))
                            ins = dve.scalar_tensor_tensor(e[:, 0, at], e[:, 0, at], sm[:, 8 + i:9 + i], e[:, 1, at],
                                                           ALU.mult, ALU.add)
                            chain.step(ins) if i < m - 1 else ins.then_inc(a_ready[layer], 1)
                    elif kind == "h_fwd":
                        _, order, s = step
                        bank = small_in(step)
                        if order == 0 and s == 0:
                            dve.wait_ge(dft_loaded[layer], 16 * 5)
                        if order * S + s:
                            last = ("h_inv", order, s - 1) if s else ("h_inv", 0, S - 1)
                            dve.wait_ge(small_done[layer], small[last] + 1)
                        re, im = [bank[:, i, :].rearrange("p (f n) -> p f n", f=2) for i in range(2)]
                        h_re, h_im = [spec[:, :, i, order * HYW:(order + 1) * HYW] for i in range(2)]
                        link(dve.tensor_tensor(htmp[:, :, :], im, h_im, ALU.mult))
                        link(dve.tensor_tensor(hprod[:, :, 0, :], re, h_re, ALU.mult))
                        link(dve.tensor_tensor(hprod[:, :, 0, :], hprod[:, :, 0, :], htmp[:, :, :], ALU.add))
                        link(dve.tensor_tensor(htmp[:, :, :], re, h_im, ALU.mult))
                        link(dve.tensor_tensor(hprod[:, :, 1, :], im, h_re, ALU.mult))
                        dve.sem_inc(free(step), 1)
                        dve.tensor_tensor(hprod[:, :, 1, :], hprod[:, :, 1, :], htmp[:, :, :], ALU.subtract)\
                            .then_inc(hprod_ready[layer], 1)
                    elif kind == "h_inv":
                        _, order, s = step
                        bank = small_in(step)
                        at = slice(s * SEQ, (s + 1) * SEQ)
                        for i in range(2):
                            skip = Bc[:, 24 + 2 * order + i:25 + 2 * order + i]
                            link(dve.scalar_tensor_tensor(htmp[:, i, :], hy[:, 2 * order + i, at], skip,
                                                          bank[:, 0, i * SEQ:(i + 1) * SEQ], ALU.mult, ALU.add))
                        dve.sem_inc(free(step), 1)
                        for i in range(2):
                            dst = hy[:, 2 + i, at] if order == 0 else hy[:, i, at]
                            ins = dve.tensor_tensor(dst, htmp[:, i, :], hy[:, 2 + 2 * order + i, at], ALU.mult)
                            if i == 1 and order == 0:
                                ins.then_inc(z_ready[layer], 1)
                                dve.wait_ge(z_ready[layer], s + 1)
                            elif i == 1 and s == S - 1:
                                ins.then_inc(yb_full[layer], 1)
                            else:
                                chain.step(ins)
                        if order == 1:
                            chain.after()
                        if order == 1 and s == S - 1:
                            dve.wait_ge(yb_hi_ready[layer], 1)
                            dve.tensor_tensor(yb_lo[:, :, 0:T], hy[:, 0:2, 0:T], yb_hi[:, :, 0:T].bitcast(F32),
                                              ALU.subtract).then_inc(yb_ready[layer], 1)
                    elif kind == "y_turn":
                        c = step[1]
                        if c == 0:
                            for i in range(nc_):
                                if i == 0:
                                    dve.wait_ge(o_ready[layer], len(units))
                                else:
                                    chain.after()
                                link(dve.tensor_tensor(tmp[:, 0:DA], o_tok[i][:, :], o_tok[i][:, :], ALU.mult))
                                chain.step(dve.tensor_reduce(ms[:, 4 * i:4 * i + 4],
                                                             tmp[:, 0:DA].rearrange("p (h n) -> p h n", n=DV),
                                                             AX.X, ALU.add))
                            chain.after()
                            dve.tensor_scalar(ms[:, 0:4 * nc_], ms[:, 0:4 * nc_], 1.0 / DV, EPS, ALU.mult, ALU.add)\
                                .then_inc(ms_ready, 1)
                            dve.wait_ge(rstd_ready, power_request(layer, "head") + 1)
                            for i in range(nc_):
                                part = o_tok[i][:, :].rearrange("p (h n) -> p h n", n=DV)
                                dve.tensor_tensor(part, part, rstd[:, 4 * i:4 * i + 4].unsqueeze(2)
                                                  .broadcast_to([P, HEADS, DV]), ALU.mult).then_inc(o_normed[layer], 1)
                        bank = small_in(step)
                        dve.wait_ge(ya_hi_ready[layer], c + 1)
                        for i in range(2):
                            at = slice((2 * c + i) * P, (2 * c + i + 1) * P)
                            ins = dve.scalar_tensor_tensor(ya_lo[:, :, at],
                                                           bank[:, i, :].rearrange("p (h n) -> p h n", h=HEADS),
                                                           Bc[:, 28:29], ya_hi[:, :, at].bitcast(F32),
                                                           ALU.mult, ALU.subtract)
                            if i == 0:
                                chain.step(ins)
                        ins.then_inc(ya_ready[layer], 1)
                        dve.wait_ge(ya_ready[layer], c + 1)
                        dve.sem_inc(free(step), 1)

                for k in range(KD):
                    dve.wait_ge(m_hi_ready[layer], k + 1)
                    dve.tensor_tensor(h_lo[:, k, 0:T], merged[:, k, 0:T], h_hi[:, k, 0:T].bitcast(F32),
                                      ALU.subtract).then_inc(m_ready[layer], 1)
                for g in range(2):
                    for j in range(4):
                        split_ahead(w)
                        w += 1
                    for m in range(4):
                        tile_in(f"o{g}", m)
                        residual(3 * layer + 1, 4 * g + m, 4 - 4 * g + m, S)

            for v in range(LOOK):
                split_low(v % SLOTS, 512, v + 1)
            for layer in range(DEPTH):
                norm(3 * layer, TOK, power_request(layer, "ffn_a"))
                ffn(2 * layer)
                norm(3 * layer + 1, TOK, power_request(layer, "mix"))
                mix(layer)
                norm(3 * layer + 2, MIX_T[layer], power_request(layer, "ffn_b"))
                ffn(2 * layer + 1)
            for c in range(2):
                dve.wait_ge(out_turned, c + 1)
                for i in range(2):
                    dve.tensor_copy(y_out[:, c, i * 512:(i + 1) * 512], ps[:, (4 if c == 0 else 0) + i, :])\
                        .then_inc(out_copied, 1)



NAMES = ["x", "c", "ctx", "c_ctx", "ada_w", "ada_b", "norm_g", "ffn_up", "ffn_down", "w_in", "da_qk_gain", "da_lambda",
         "da_subln", "hy_conv_w", "hy_conv_b", "hy_f_w1", "hy_f_b1", "hy_f_w2", "hy_f_b2", "hy_f_freq", "hy_f_w3",
         "hy_skip", "sg_ln_g", "sg_ln_b", "sg_w", "sg_b", "gate_w", "gate_b", "w_br", "w_o"]


def shape_constants():
    n = SEQ
    f32 = np.float32
    time = np.linspace(0.0, 1.0, n)[:, None]
    w = (2.0 * math.pi / n) * np.arange(n)[:, None]
    bands = np.linspace(1e-4, (EMB - 1) // 2 - 1, (EMB - 1) // 2)
    pos = np.concatenate([time, np.cos(bands * w), -np.sin(bands * w)], axis=-1).T
    deltas = np.linspace(math.log(1e-2) / 1.5, math.log(1e-2) / 0.3, 2 * HYW)
    decay = np.repeat(np.exp(-time * np.abs(deltas))[:, None, :], 2, axis=1)
    decay[0, 1] = 0.0
    angle = (2.0 * math.pi / (2 * n)) * np.outer(np.arange(n), np.arange(n) + 0.5)
    fwd = np.stack([np.cos(angle), np.sin(angle)], axis=1)
    inv = np.stack([np.cos(angle).T, np.sin(angle).T], axis=1) / n
    inv_f = 10000.0 ** (-np.arange(16) / 16)
    at = np.arange(n)
    ang = (np.stack([at // GRID_W, at % GRID_W], axis=-1)[:, :, None] * inv_f).reshape(n, 32)
    return {"filter_pos": pos.astype(f32), "decay": decay.astype(f32), "dft": np.stack([fwd, inv]).astype(f32),
            "rope": np.stack([np.cos(ang), np.sin(ang)], axis=1).astype(f32), "ident": np.eye(P, dtype=f32)}


def kernel(**inputs):
    import concourse.bacc as bacc
    from concourse.bass_utils import run_bass_kernel_spmd
    arrays = {name: np.ascontiguousarray(inputs[name]) for name in NAMES} | shape_constants()
    nc = bacc.Bacc("TRN2", target_bir_lowering=False, num_devices=1)
    t = {name: nc.dram_tensor(f"in_{name}", a.shape, F32, kind="ExternalInput").ap() for name, a in arrays.items()}
    out = nc.dram_tensor("out_0", (SEQ, D), F32, kind="ExternalOutput").ap()
    build(nc, t, out)
    r = run_bass_kernel_spmd(nc, [{f"in_{name}": a for name, a in arrays.items()}], core_ids=[0])
    return r.results[0]["out_0"].reshape(1, SEQ, D)
```

```python
from contextlib import ExitStack
import math

import numpy as np

import concourse.bass as bass
from concourse import mybir

F32 = mybir.dt.float32
F32R = mybir.dt.float32r
ACT = mybir.ActivationFunctionType
ALU = mybir.AluOpType
AX = mybir.AxisListType

P = 128
D = 1024
KD = D // P
SEQ = 256
TOK = 512
NT = TOK // P
DEPTH = 2
N_MOD = 9
FFN = 2816
KF = FFN // P
EPS = 1e-6

HEADS, DH, DV = 4, 64, 128
DA = HEADS * DV
HYW = 256
SGW = 256
HY_OFF = 3 * DA
SG_OFF = HY_OFF + 3 * HYW
GRID_W = 64
EMB, FH = 33, 64

SLOTS = 4
LOOK = 3
UP_GROUPS = FFN // 256
DOWN_PAIRS = KF // 2
FFN_PAIRS = 4 * UP_GROUPS + 2 * DOWN_PAIRS
ADA_GROUPS = N_MOD * D // 512
ADA_START = 4
WARM = (4, 8)
ADDED = 5
FIRST_ADA = 3
COLS_A, COLS_B = 120, 32


def lam_init(layer):
    return 0.8 - 0.6 * math.exp(-0.3 * layer)


def up_tiles():
    return (0, 256, 128, 384)


def banks_of(group):
    return (0, 1, 2, 3) if group % 2 == 0 else (4, 5, 6, 3)


class Chain:

    def __init__(self, eng, sem):
        self.eng, self.sem, self.n = eng, sem, 0

    def step(self, ins):
        self.n += 1
        return ins.then_inc(self.sem, 1)

    def after(self, back=0):
        self.eng.wait_ge(self.sem, self.n - back)



def mix_gemms(layer):
    out = [("k", "w_in", 0, DA, 4, 512), ("q", "w_in", 0, 0, 4, 512), ("v", "w_in", 0, 2 * DA, 4, 512),
           ("sgv", "w_in", 0, SG_OFF + SGW, 4, 256),
           ("f0", "w_in", 0, HY_OFF, 4, 512), ("f1", "w_in", 0, HY_OFF + 512, 4, 512)]
    for branch, gate, row, pairs in (("c", 2, DA + HYW, 1), ("b", 1, DA, 1), ("a", 0, 0, 2)):
        gates = [(f"gate_{branch}{g}", "gate_w", 0, gate * D + g * 512, 4, 512) for g in range(2)]
        projections = [(f"br_{branch}{g}", "w_br", row, g * 512, pairs, 512) for g in range(2)]
        out += gates + projections if branch == "a" else [gates[0], projections[0], gates[1], projections[1]]
    out += [(f"o{g}", "w_o", 0, g * 512, 4, 512) for g in range(2)]
    return out


MIX_PAIRS = sum(g[4] for g in mix_gemms(0))


def softmax_units(streams):
    units = [((qc,), 0, h) for qc in range(2) for h in range(HEADS)]
    if streams == 2:
        units += [((2, 3), 2, h) for h in range(HEADS)]
    return units


def mix_schedule(streams):
    gemms = mix_gemms(0)[4:-2]
    pairs = [(g[0], j) for g in gemms for j in range(g[4])]
    gaps = [[] for _ in pairs]
    first_a, first_b = pairs.index(("br_a0", 0)), pairs.index(("br_b0", 0))
    gaps[0] += [("qk_turn", 0)]
    gaps[1] += [("qk_turn", 1), ("qk_turn", 2)]
    gaps[2] += [("qk_turn", 3)]
    units = softmax_units(streams)
    at, weights = 2, {}
    for u in range(len(units)):
        gaps[at] += [("scores", u)]
        weights.setdefault(at + 1, []).append(("weights", u))
        gaps[at + 3] += [("turn", u)]
        gaps[at + 4] += [("mixv", u)]
        if u % 8 == 7 or u == len(units) - 1:
            weights.setdefault(at + 4, []).append(("heads", u // 8))
            gaps[at + 5] += [("y_turn", u // 8)]
            assert at + 5 < first_a
        at += 3 if u < 6 else 2
    hyena = []
    for order in range(2):
        hyena += [("h_turn", order)]
        for s in range(streams):
            hyena += [("h_fwd", order, s), ("h_inv", order, s)]
    gaps[3] += [("ws_turn",)]
    gaps[5] += [("sg_mix",)]
    at = 6
    for step in hyena:
        gaps[at] += [step]
        at += 2 if at % 3 else 1
        assert at < first_b
    for gap, steps in weights.items():
        gaps[gap] += steps
    order = []
    for (name, j), steps in zip(pairs, gaps):
        order.append(("pair", name, j))
        if (name, j + 1) not in pairs:
            order.append(("drain", name))
        order += steps
    return order


def small_products(schedule):
    names = [s for s in schedule if s[0] not in ("pair", "drain", "weights", "heads")]
    return {s: n for n, s in enumerate(names)}



def build(nc, t, out):
    ctx = ExitStack()
    with ctx:
        place_at = [16640]

        def sb(name, shape, dt=F32, at=None):
            size = -(-math.prod(shape[1:]) * 4 // 32) * 32
            where = place_at[0] if at is None else at
            if at is None:
                place_at[0] += size
            assert where + size <= 229344, (name, where + size)
            return nc.alloc_sbuf_tensor_at(name, shape, dt, offset=where)

        def sem(name):
            return ctx.enter_context(nc.semaphore(name))

        x = sb("x", [P, KD, TOK])
        h_hi = sb("h_hi", [P, KD, TOK], F32R)
        h_lo_at = place_at[0]
        h_lo = sb("h_lo", [P, KD, TOK], F32R)
        raw = sb("raw", [P, SLOTS, 1024])
        w_hi = sb("w_hi", [P, SLOTS, 1024], F32R)
        w_lo = sb("w_lo", [P, SLOTS, 1024], F32R)
        ident = sb("ident", [P, P])
        ones = sb("ones", [P, P])
        prm = sb("prm", [P, DEPTH, COLS_A + COLS_B])
        mod = sb("mod", [P, DEPTH, N_MOD * KD, 2])
        mod_a = sb("mod_a", [P, 3 * DEPTH, KD, 2])
        mod_g = sb("mod_g", [P, 3 * DEPTH, KD, 2])
        sil_c = sb("sil_c", [P, KD, 2])
        lam = sb("lam", [P, DEPTH])
        ada_bias = sb("ada_bias", [P, DEPTH * N_MOD * KD])
        half_pow = sb("half_pow", [P, 8])
        ms = sb("ms", [P, 64])
        rstd = sb("rstd", [P, 64])
        arena = place_at[0]

        u_hi = sb("u_hi", [P, KF, TOK], F32R)
        u_lo = sb("u_lo", [P, KF, TOK], F32R)
        ada_raw = sb("ada_raw", [P, 2, 1024])
        ada_acc = sb("ada_acc", [P, 2, 512])
        uf = sb("uf", [P, 2, TOK])
        ffn_end = place_at[0]
        sq_h = sb("sq_h", [P, KD, TOK], at=h_lo_at)
        sq_m = sb("sq_m", [P, KD, TOK], at=arena)
        hf = sb("hf", [P, 3, TOK], at=arena)
        diag = sb("diag", [P, TOK], at=arena + 6144)
        y_out = sb("y_out", [P, 2, D], at=h_lo_at)

        place_at[0] = arena + 8192
        ada0 = sb("ada0", [P, ADA_START, KD * 512])
        acc0 = sb("acc0", [P, 2, 512])
        prow = sb("prow", [P, DEPTH, 2, P])
        crow = sb("crow", [2 * KD, P])
        lv = sb("lv", [P, DEPTH, 4, DH])
        rows2 = sb("rows2", [2, ADA_START - 1, 512])
        lsum = sb("lsum", [P, 2 * DEPTH])
        assert place_at[0] <= arena + 2 * KF * TOK * 4

        place_at[0] = arena + 10 * TOK * 4
        decay = sb("decay", [P, 2, 2, 512])
        taps = sb("taps", [P, 2, 2, 512])
        spec0 = taps
        tmag = sb("tmag", [P, 2, 2, 512])
        assert place_at[0] <= arena + KF * TOK * 4
        place_at[0] = arena + (KF + 10) * TOK * 4
        dft_f0 = sb("dft_f0", [P, 2, 2, SEQ])
        inv_l1 = sb("inv_l1", [P, 512])
        zt = sb("zt", [EMB, SEQ])
        fw1 = sb("fw1", [EMB, FH])
        fw2 = sb("fw2", [FH, FH])
        fw3 = sb("fw3", [FH, 1024])
        f_arg = sb("f_arg", [FH, SEQ])
        f_turns = sb("f_turns", [FH, SEQ])
        f_sin = sb("f_sin", [FH, 2, SEQ])
        assert place_at[0] <= arena + 2 * KF * TOK * 4

        place_at[0] = arena
        r1 = place_at[0]
        qk = sb("qk", [P, NT, 1024])
        dft = sb("dft", [P, 2, 2, 2, SEQ], at=r1)
        spec = sb("spec", [P, 2, 2, 512], at=r1 + 8192)
        ya_hi = sb("ya_hi", [P, HEADS, TOK], F32R, at=r1)
        ya_lo = sb("ya_lo", [P, HEADS, TOK], F32R, at=r1 + 8192)
        vtok = sb("vtok", [P, NT, DA])
        qT = sb("qT", [P, HEADS, TOK])
        kT = sb("kT", [P, HEADS, TOK])
        e_at = place_at[0]
        e = sb("e", [P, 2, 512])
        tmp = sb("tmp", [P, 1024], at=e_at)
        aT = sb("aT", [P, 512])
        gate_at = place_at[0]
        gate = sb("gate", [P, 4, TOK])
        ws = sb("ws", [P, 4, P], at=gate_at)
        merged_at = place_at[0]
        merged = sb("merged", [P, KD, TOK])
        hy_at = place_at[0]
        hy = sb("hy", [P, 6, TOK])
        yb_lo = sb("yb_lo", [P, 2, TOK], F32R, at=hy_at)
        yb_hi = sb("yb_hi", [P, 2, TOK], F32R, at=hy_at + 4096)
        gate_a1 = sb("gate_a1", [P, 4, TOK], at=hy_at)
        u_raw = [sb(f"u_raw{c}", [P, TOK], at=merged_at + (c if c < 4 else c + 2) * TOK * 4) for c in range(6)]
        sgu_at = place_at[0]
        sgu = sb("sgu", [P, 2, TOK])
        yc_lo = sb("yc_lo", [P, 2, TOK], F32R, at=sgu_at)
        yc_at = place_at[0]
        yc_hi = sb("yc_hi", [P, 2, TOK], F32R)
        sgm = sb("sgm", [P, 2, TOK], at=yc_at)
        sgv_at = place_at[0]
        sgv = sb("sgv", [P, NT, SGW])
        htok = sb("htok", [P, NT, HYW], at=sgv_at)
        hprod_at = place_at[0]
        hprod = sb("hprod", [P, 2, 2, HYW])
        htmp = sb("htmp", [P, 2, HYW])
        o0 = sb("o0", [P, DA])
        o_tok = [o0, sb("o1", [P, DA], at=yc_at), sb("o2", [P, DA], at=yc_at + 2048),
                 sb("o3", [P, DA], at=sgu_at)]
        e_merged = sb("e_merged", [P, 2, 512], at=merged_at + 4 * TOK * 4)
        e_sgu = sb("e_sgu", [P, 2, 512], at=sgu_at)
        e_hprod = sb("e_hprod", [P, 2, 512], at=hprod_at)

        def exps_of(u):
            if u % 2 == 0:
                return e
            return e_merged if u < 5 else e_sgu if u < 8 else e_hprod
        rope = sb("rope", [P, 2, 2, 32])
        qk_gain = sb("qk_gain", [P, 2, DH])
        ln_g = sb("ln_g", [P, SGW])
        ln_b = sb("ln_b", [P, SGW])
        sgb = sb("sgb", [P, 2, P])
        wsT = sb("wsT", [P, 4, P], at=hprod_at)
        sm = sb("sm", [P, 2, 16])
        stats = sb("stats", [P, NT, 8])
        head_sq = sb("head_sq", [P, NT * HEADS])
        mix_end = place_at[0]

        ps = ctx.enter_context(nc.psum_tensor("ps", [P, 8, 512], F32))
        MISC = 7
        spectra = nc.dram_tensor("hyena_spectra", [DEPTH, P, 2 * 2 * 512], F32, kind="Internal").ap()

        raw_loaded = [sem(f"raw_loaded{i}") for i in range(SLOTS)]
        hi_ready = sem("hi_ready")
        lo_ready = sem("lo_ready")
        pair_used = sem("pair_used")
        const_loaded = sem("const_loaded")
        row_loaded = sem("row_loaded")
        c_loaded = sem("c_loaded")
        c_turned = sem("c_turned")
        row_cleared = sem("row_cleared")
        flt_loaded = sem("flt_loaded")
        ada0_loaded = [sem(f"ada0_loaded{i}") for i in range(ADA_START)]
        ones_set = sem("ones_set")
        turned = sem("turned")
        prm_ready = sem("prm_ready")
        sil_ready = sem("sil_ready")
        xt_done = sem("xt_done")
        x0_ready = sem("x0_ready")
        ada0_done = sem("ada0_done")
        acc0_step = sem("acc0_step")
        rows2_done = sem("rows2_done")
        rows2_out = sem("rows2_out")
        squares_added = sem("squares_added")
        flt_pe = sem("flt_pe")
        flt_v = sem("flt_v")
        flt_a = sem("flt_a")
        spec_stored = sem("spec_stored")
        lv_loaded = sem("lv_loaded")
        lam_v = sem("lam_v")
        lam_a = sem("lam_a")
        x_ready = sem("x_ready")
        squared = sem("squared")
        sums_done = sem("sums_done")
        ms_ready = sem("ms_ready")
        rstd_ready = sem("rstd_ready")
        diag_ready = sem("diag_ready")
        rstd_spread = sem("rstd_spread")
        hf_step = sem("hf_step")
        h_hi_ready = sem("h_hi_ready")
        h_ready = sem("h_ready")
        mod_step = sem("mod_step")
        tile_done = [sem(f"tile_done{f}") for f in range(4)]
        sil_a = sem("sil_a")
        uf_ready = sem("uf_ready")
        u_hi_ready = sem("u_hi_ready")
        u_ready = sem("u_ready")
        ada_loaded = [sem(f"ada_loaded{i}") for i in range(2)]
        ada_step = sem("ada_step")
        ada_folded = sem("ada_folded")
        ada_taken = sem("ada_taken")
        def by_layer(name):
            return [sem(f"{name}_{layer}") for layer in range(DEPTH)]

        mix_done = by_layer("mix_done")
        drained = [{g[0]: sem(f"drained_{g[0]}_{layer}") for g in mix_gemms(layer)[:-2]} for layer in range(DEPTH)]
        taps_done = by_layer("taps_done")
        small_done = by_layer("small_done")
        slot_free = [[sem(f"slot_free{b}_{layer}") for b in range(2)] for layer in range(DEPTH)]
        mixc_loaded = sem("mixc_loaded")
        dft_loaded = sem("dft_loaded")
        conv_ready = by_layer("conv_ready")
        z_ready = by_layer("z_ready")
        qk_normed = by_layer("qk_normed")
        ln_done = by_layer("ln_done")
        ws_ready = sem("ws_ready")
        qkT_ready = by_layer("qkT_ready")
        yc_full = by_layer("yc_full")
        yc_hi_ready = by_layer("yc_hi_ready")
        yc_ready = by_layer("yc_ready")
        yb_full = sem("yb_full")
        yb_hi_ready = sem("yb_hi_ready")
        yb_ready = sem("yb_ready")
        ya_hi_ready = by_layer("ya_hi_ready")
        ya_ready = by_layer("ya_ready")
        htok_ready = by_layer("htok_ready")
        hprod_ready = by_layer("hprod_ready")
        max_ready = by_layer("max_ready")
        exp_ready = by_layer("exp_ready")
        a_ready = by_layer("a_ready")
        aT_ready = by_layer("aT_ready")
        o_ready = by_layer("o_ready")
        o_normed = by_layer("o_normed")
        merged_added = sem("merged_added")
        m_hi_ready = by_layer("m_hi_ready")
        m_ready = by_layer("m_ready")
        v_step = sem("v_step")
        out_turned = sem("out_turned")
        out_copied = sem("out_copied")
        out_copied_a = sem("out_copied_a")
        out_stored = sem("out_stored")

        ffn_first = []
        mix_first = []
        w = 0
        for layer in range(DEPTH):
            ffn_first.append(w)
            w += FFN_PAIRS
            mix_first.append(w)
            w += MIX_PAIRS
            ffn_first.append(w)
            w += FFN_PAIRS
        N_PAIRS = w
        FFNS = [(0, 0, TOK), (0, 2, TOK), (1, 0, TOK), (1, 2, SEQ)]
        MIX_T = [TOK, SEQ]
        ADA_UP = UP_GROUPS - FIRST_ADA
        ADA_DOWN = [(2, 2), (2, 0), (2, 0), (0, 0)]
        ADA_FFN_GROUPS = [(ADA_UP if sum(d) else 0) + sum(d) for d in ADA_DOWN]
        ADA_FFN_FIRST = [sum(ADA_FFN_GROUPS[:f]) for f in range(4)]
        assert ADA_START + sum(ADA_FFN_GROUPS) == DEPTH * ADA_GROUPS

        FILTER_AT = {(0, 3): ([], [0]), (1, 0): ([], [1]), (1, 1): ([2], [3]), (1, 2): ([4], [5]), (1, 3): ([], [6]),
                     (2, 0): ([], [7]), (2, 1): ([8], [9]), (2, 2): ([10], [])}

        def filter_steps(f, g, j):
            return FILTER_AT.get((g, j), ([], [])) if f < DEPTH and isinstance(g, int) else ([], [])

        def ada_src(q, k0, k1):
            layer, g = q // ADA_GROUPS, q % ADA_GROUPS
            return t["ada_w"][layer, k0 * P:k1 * P, g * 512:(g + 1) * 512].rearrange("(k p) n -> p k n", p=P)

        def mix_gemm(layer, name):
            w = mix_first[layer]
            for g in mix_gemms(layer):
                if g[0] == name:
                    return w, g
                w += g[4]

        block = ctx.enter_context(nc.Block())

        @block.sync
        def _(sp):
            sp.dma_start(ident[:, :], t["ident"]).then_inc(const_loaded, 16)
            for c in range(NT):
                src = (t["x"][0] if c < 2 else t["ctx"][0])[(c % 2) * P:(c % 2 + 1) * P, :]
                for k in range(2):
                    sp.dma_start(raw[:, c, k * 512:(k + 1) * 512], src[:, k * 512:(k + 1) * 512])\
                        .then_inc(raw_loaded[c], 16)
            for q in (0, 2, 1, 3):
                if q == 1:
                    sp.wait_ge(row_loaded, 160)
                sp.dma_start(ada0[:, q, :].rearrange("p (k n) -> p k n", k=KD), ada_src(q, 0, KD))\
                    .then_inc(ada0_loaded[q], 16)

            def load_up(slot, w_up, j, col):
                for k in range(2):
                    rows = w_up[(2 * j + k) * P:(2 * j + k + 1) * P, :].rearrange("p (s n) -> p s n", s=2)
                    sp.dma_start(raw[:, slot, k * 512:(k + 1) * 512].rearrange("p (s n) -> p s n", s=2),
                                 rows[:, :, col]).then_inc(raw_loaded[slot], 16)

            def load_rows(slot, matrix, row, col, cols):
                for k in range(2):
                    sp.dma_start(raw[:, slot, k * 512:k * 512 + cols],
                                 matrix[bass.ds(row + k * P, P), col:col + cols]).then_inc(raw_loaded[slot], 16)

            def load_ffn(f):
                layer, which, w0 = f // 2, f % 2, ffn_first[f]
                w_up, w_down = t["ffn_up"][layer, which], t["ffn_down"][layer, which]
                first = 0
                if f == 0:
                    sp.wait_ge(x0_ready, 2 * NT)
                    for j in range(4):
                        load_up((w0 + j) % SLOTS, w_up, j, slice(0, 256))
                    first = 1
                with sp.Fori(first, UP_GROUPS) as g:
                    for j in range(4):
                        sp.wait_ge(lo_ready, g * 4 + (w0 + j - SLOTS + 1))
                        load_up((w0 + j) % SLOTS, w_up, j, bass.ds(g * 256, 256))
                for half in range(2):
                    wd = w0 + 4 * UP_GROUPS + half * DOWN_PAIRS
                    with sp.Fori(0, DOWN_PAIRS // 4) as i:
                        for j in range(4):
                            sp.wait_ge(lo_ready, i * 4 + (wd + j - SLOTS + 1))
                            load_rows((wd + j) % SLOTS, w_down, i * 1024 + j * 256, half * 512, 512)
                    for j in range(DOWN_PAIRS // 4 * 4, DOWN_PAIRS):
                        sp.wait_ge(lo_ready, wd + j - SLOTS + 1)
                        load_rows((wd + j) % SLOTS, w_down, j * 256, half * 512, 512)

            def load_mix(layer):
                w = mix_first[layer]
                for _, weight, row, col, pairs, cols in mix_gemms(layer):
                    for j in range(pairs):
                        sp.wait_ge(lo_ready, w - SLOTS + 1)
                        load_rows(w % SLOTS, t[weight][layer], row + j * 256, col, cols)
                        w += 1

            for layer in range(DEPTH):
                load_ffn(2 * layer)
                load_mix(layer)
                load_ffn(2 * layer + 1)
            for c, i in ((0, 0), (1, 0), (0, 1), (1, 1)):
                if (c, i) == (1, 1):
                    sp.wait_ge(out_copied_a, 1)
                else:
                    sp.wait_ge(out_copied, 2 * i + c + 1)
                sp.dma_start(out[c * P:(c + 1) * P, i * 512:(i + 1) * 512],
                             y_out[:, c, i * 512:(i + 1) * 512]).then_inc(out_stored, 16)
            sp.wait_ge(out_stored, 64)

        SCHED = [mix_schedule(T // SEQ) for T in MIX_T]
        SMALL = [small_products(s) for s in SCHED]
        UNITS = [softmax_units(T // SEQ) for T in MIX_T]
        GEMM_AT = {g[0]: n for n, g in enumerate(mix_gemms(0))}
        N_CHUNKS = [T // P for T in MIX_T]
        N_ROWS = 10

        def in_tiles(layer, name):
            if name in ("q", "sgv"):
                return N_CHUNKS[layer]
            return 4

        def wait_tile(eng, layer, name, i):
            n, w = 0, mix_first[layer]
            for g in mix_gemms(layer):
                tiles = in_tiles(layer, g[0])
                if g[0] == name:
                    break
                n, w = n + tiles - 1, w + g[4]
            if i == tiles - 1:
                eng.wait_ge(pair_used, w + g[4])
            else:
                eng.wait_ge(mix_done[layer], n + i + 1)

        POWERS = [["ffn_a", "mix"] + [f"k{c}" for c in range(NT)] + [f"q{c}" for c in range(T // P)] + ["ln"] +
                  [f"head{s}" for s in range(T // SEQ)] + ["ffn_b"] for T in MIX_T]

        def power_request(layer, what):
            return sum(len(p) for p in POWERS[:layer]) + POWERS[layer].index(what)

        FLT_V, FLT_P, FLT_A = 25, 11, 6
        FLT_V_BEFORE = (0, 7, 14, 15, 16, 17, 18, 21, 22, 23, 24, 25)

        def HF_FULL(n, k):
            return 24 * n + (3 if n < 5 else 2) * (k + 1)

        def pair_cols(w):
            for layer in range(DEPTH):
                first = mix_gemm(layer, "sgv")[0]
                if first <= w < first + 4:
                    return SGW
            return 512

        @block.gpsimd
        def _(pool):
            pool.memset(prow[:, :, :, :], 0.0).then_inc(row_cleared, 1)
            pool.memset(ones[:, :], 1.0).then_inc(ones_set, 1)
            pool.memset(half_pow[:, :], -0.5).then_inc(ones_set, 1)
            pool.wait_ge(row_cleared, 1)
            for block, row, rows, src in (
                    (0, 0, 72, t["ada_b"].rearrange("l (r p) -> r l p", p=P)),
                    (0, 72, 24, t["norm_g"].rearrange("l i (k p) -> (i k) l p", p=P)),
                    (0, 96, 24, t["gate_b"].rearrange("l (r p) -> r l p", p=P)),
                    (1, 0, 18, t["hy_conv_w"].rearrange("l i (k p) -> (i k) l p", p=P)),
                    (1, 18, 6, t["hy_conv_b"].rearrange("l (r p) -> r l p", p=P)),
                    (1, 24, 4, t["hy_skip"].rearrange("l i (k p) -> (i k) l p", p=P)),
                    (1, 28, 1, t["da_subln"].rearrange("l (r p) -> r l p", p=P))):
                pool.dma_start(prow[row:row + rows, :, block, :], src).then_inc(row_loaded, 16)
            for i, name in enumerate(("hy_f_b1", "hy_f_b2", "hy_f_freq")):
                pool.dma_start(prow[29 + i:30 + i, :, 1, 0:FH], t[name].rearrange("l (r p) -> r l p", p=FH))\
                    .then_inc(row_loaded, 16)
            pool.dma_start(lv[:, :, :, :].rearrange("p l i n -> p (l i n)"),
                          t["da_lambda"].rearrange("l i n -> (l i n)").partition_broadcast(P)).then_inc(lv_loaded, 16)
            pool.wait_ge(ones_set, 2)

            def power(request, cols, first=0):
                pool.wait_ge(ms_ready, request + 1)
                pool.tensor_tensor(rstd[:, first:first + cols], ms[:, first:first + cols], half_pow[:, 0:cols], ALU.pow)\
                    .then_inc(rstd_ready, 1)

            def add_squares(n, T, squares):
                for k in range(1, ADDED):
                    pool.wait_ge(squared, KD * n + k + 1)
                    if k > 1:
                        pool.wait_ge(squares_added, (ADDED - 1) * n + k - 1)
                    pool.tensor_tensor(squares[:, 0, 0:T], squares[:, 0, 0:T], squares[:, k, 0:T], ALU.add)\
                        .then_inc(squares_added, 1)

            def load_filter(layer):
                if layer == 0:
                    pool.wait_ge(mod_step, ADA_START)
                    pool.wait_ge(lam_v, 2 * DEPTH)
                else:
                    pool.wait_ge(m_ready[layer - 1], KD)
                n = flt_loaded
                pool.dma_start(zt[:, :], t["filter_pos"]).then_inc(n, 16)
                pool.dma_start(fw1[:, :], t["hy_f_w1"][layer]).then_inc(n, 16)
                pool.dma_start(fw2[:, :], t["hy_f_w2"][layer]).then_inc(n, 16)
                pool.dma_start(fw3[:, :], t["hy_f_w3"][layer]).then_inc(n, 16)
                pool.dma_start(decay[:, :, :, :].rearrange("p c a b -> p c (a b)"),
                               t["decay"].rearrange("(c p) a b -> p c (a b)", p=P)).then_inc(n, 16)
                pool.dma_start(dft_f0[:, :, :, :].rearrange("p c a b -> p c (a b)"),
                               t["dft"][0].rearrange("(c p) a b -> p c (a b)", p=P)).then_inc(n, 16)

            def store_spectrum(layer):
                pool.wait_ge(flt_v, FLT_V * (layer + 1))
                pool.dma_start(spectra[layer], spec0[:, :, :, :].rearrange("p a b c -> p (a b c)"))\
                    .then_inc(spec_stored, 16)

            def load_ada(f):
                first, groups = ADA_FFN_FIRST[f], ADA_FFN_GROUPS[f]
                q0 = ADA_START + first
                runs, q = [], q0
                while q < q0 + groups:
                    stop = min(q0 + groups, (q // ADA_GROUPS + 1) * ADA_GROUPS)
                    runs.append((q, stop))
                    q = stop
                for a, b in runs:
                    w_ada, col = t["ada_w"][a // ADA_GROUPS], (a % ADA_GROUPS) * 512
                    v0 = 4 * (a - ADA_START)

                    def unit(i, j, wait):
                        if wait is not None:
                            pool.wait_ge(ada_step, wait)
                        src = w_ada[2 * j * P:(2 * j + 2) * P, bass.ds(i * 512 + col, 512)]
                        pool.dma_start(ada_raw[:, j % 2, :].rearrange("p (k n) -> p k n", k=2),
                                       src.rearrange("(k p) n -> p k n", p=P)).then_inc(ada_loaded[j % 2], 16)

                    first_run = v0 == 0
                    if first_run:
                        for j in range(4):
                            unit(0, j, 4 * (j - 1) if j >= 2 else None)
                    with pool.Fori(1 if first_run else 0, b - a) as i:
                        for j in range(4):
                            unit(i, j, i * 16 + 4 * (v0 + j - 1))

            def load_mix_constants(layer):
                pool.wait_ge(pair_used, mix_first[layer])
                n = mixc_loaded
                pool.dma_start(rope[:, :, :, :].rearrange("p c a b -> p c (a b)"),
                               t["rope"].rearrange("(c p) a b -> p c (a b)", p=P)).then_inc(n, 16)
                pool.dma_start(qk_gain[:, :, :], t["da_qk_gain"][layer].partition_broadcast(P)).then_inc(n, 16)
                pool.dma_start(ln_g[:, :], t["sg_ln_g"][layer:layer + 1, :].rearrange("a b -> (a b)")
                               .partition_broadcast(P)).then_inc(n, 16)
                pool.dma_start(ln_b[:, :], t["sg_ln_b"][layer:layer + 1, :].rearrange("a b -> (a b)")
                               .partition_broadcast(P)).then_inc(n, 16)
                for g in range(4):
                    pool.dma_start(sgb[64 * (g % 2):64 * (g % 2) + 64, g // 2, :],
                                   t["sg_b"][layer, g].partition_broadcast(64)).then_inc(n, 16)
                pool.dma_start(ws[:, :, :], t["sg_w"][layer].rearrange("g i j -> i g j")).then_inc(n, 16)

            def add_branch(layer, name):
                T = MIX_T[layer]
                for i in range(4):
                    pool.wait_ge(drained[layer][name], i + 1)
                    part = merged[:, 4 * int(name[4]) + i, 0:T]
                    gated = (gate_a1 if name == "br_a1" else gate)[:, i, 0:T]
                    pool.tensor_tensor(part, part, gated, ALU.add).then_inc(merged_added, 1)

            def load_dft(layer):
                pool.wait_ge(qkT_ready[layer], 4)
                for way in range(2):
                    for c in range(2):
                        pool.dma_start(dft[:, c, way, :, :], t["dft"][way, c * P:(c + 1) * P]).then_inc(dft_loaded, 16)
                pool.wait_ge(spec_stored, 16 * (layer + 1))
                pool.dma_start(spec[:, :, :, :].rearrange("p a b c -> p (a b c)"), spectra[layer])\
                    .then_inc(dft_loaded, 16)

            for layer in range(DEPTH):
                add_squares(3 * layer, TOK, sq_h)
                power(power_request(layer, "ffn_a"), NT)
                if layer == 0:
                    load_filter(0)
                    store_spectrum(0)
                load_ada(2 * layer)
                add_squares(3 * layer + 1, TOK, sq_h)
                power(power_request(layer, "mix"), NT)
                load_mix_constants(layer)
                for name in ("k", "q"):
                    for c in range(NT if name == "k" else N_CHUNKS[layer]):
                        power(power_request(layer, f"{name}{c}"), 8, 16 * c + 8 * (name == "k"))
                power(power_request(layer, "ln"), NT)
                load_dft(layer)
                for step in SCHED[layer]:
                    if step[0] == "heads":
                        power(power_request(layer, f"head{step[1]}"), 8)
                    elif step in (("drain", "br_b0"), ("drain", "br_b1"), ("drain", "br_a0"), ("drain", "br_a1")):
                        add_branch(layer, step[1])
                if layer == 0:
                    load_filter(1)
                add_squares(3 * layer + 2, MIX_T[layer], sq_m)
                power(power_request(layer, "ffn_b"), NT)
                if layer == 0:
                    store_spectrum(1)
                    load_ada(1)

        @block.scalar
        def _(act):
            act.dma_start(crow[0:KD, :], t["c"].rearrange("a (k p) -> (a k) p", p=P)).then_inc(c_loaded, 16)
            act.dma_start(crow[KD:, :], t["c_ctx"].rearrange("(k p) -> k p", p=P)).then_inc(c_loaded, 16)

            act.wait_ge(c_turned, 1)
            act.activation(sil_c[:, :, :].rearrange("p k s -> p s k"),
                           ps[:, 6, 0:2 * KD].rearrange("p (s k) -> p s k", s=2), ACT.Silu).then_inc(sil_ready, 1)
            def filter_step(layer, step):
                if step < 6:
                    act.wait_ge(flt_v, FLT_V * layer + FLT_V_BEFORE[step + 1])
                if step < 2:
                    act.activation(f_sin[:, step, :], f_arg[:, :], ACT.Sin).then_inc(flt_a, 1)
                elif step < 6:
                    c, way = (step - 2) // 2, step % 2
                    act.activation(tmag[:, c, way, :], taps[:, c, way, :], ACT.Abs).then_inc(flt_a, 1)

            def split_high(w, slot, cols=512, wait=None, free=None):
                act.wait_ge(raw_loaded[slot], wait)
                if free is not None:
                    act.wait_ge(pair_used, free)
                src = raw[:, slot, :].rearrange("p (k n) -> p k n", k=2)[:, :, 0:cols]
                dst = w_hi[:, slot, :].rearrange("p (k n) -> p k n", k=2)[:, :, 0:cols]
                act.activation(dst, src, ACT.Copy).then_inc(hi_ready, 1)

            def split_ahead(w):
                v = w + LOOK
                if v < N_PAIRS:
                    split_high(v, v % SLOTS, pair_cols(v), 32 * (v // SLOTS + 2),
                               v - SLOTS + 1 if v >= SLOTS else None)

            def split_ahead_in_loop(w0, j, turns, i):
                v = w0 + j + LOOK
                split_high(v, v % SLOTS, 512, i * (32 * turns // SLOTS) + 32 * (v // SLOTS + 2),
                           i * turns + (v - SLOTS + 1))

            def copy_rows2(i):
                act.wait_ge(rows2_done, i + 1)
                act.activation(rows2[:, i, :], ps[0:2, 4 + i, :], ACT.Copy).then_inc(rows2_out, 1)

            def norm(n, T, squares):
                for k in range(KD):
                    if n == 0:
                        act.wait_ge(x0_ready, 2 * NT)
                    else:
                        act.wait_ge(x_ready, KD * (n - 1) + k + 1)
                    act.activation(squares[:, k, 0:T], x[:, k, 0:T], ACT.Square).then_inc(squared, 1)
                if n == 0:
                    act.wait_ge(lam_v, 2 * DEPTH)
                    act.activation(lsum[:, :], lsum[:, :], ACT.Exp).then_inc(lam_a, 1)
                    copy_rows2(0)
                    copy_rows2(1)
                    for v in range(LOOK):
                        split_high(v, v % SLOTS, 512, 32 * (v // SLOTS + 2))
                    copy_rows2(2)
                for k in range(KD):
                    act.wait_ge(hf_step, HF_FULL(n, k))
                    act.activation(h_hi[:, k, 0:T], hf[:, k % 3, 0:T], ACT.Copy).then_inc(h_hi_ready, 1)

            def ffn(f):
                layer, sub, T = FFNS[f]
                w0 = ffn_first[f]

                def drain_up(g, parity):
                    banks = banks_of(parity)
                    for i in range(2):
                        act.wait_ge(tile_done[f], g * 3 + (2 * i + 1))
                        if not (f == 0 and isinstance(g, int) and g == 0):
                            act.wait_ge(u_ready, g * 2 + (KF * f + i - 1))
                        act.activation(uf[:, i, 0:T], ps[:, banks[2 * i], 0:T], ACT.Silu).then_inc(sil_a, 1)
                    for i in range(2):
                        act.wait_ge(uf_ready, g * 2 + (KF * f + i + 1))
                        dst = u_hi[:, bass.ds(g * 2 + i, 1), 0:T] if not isinstance(g, int) else u_hi[:, 2 * g + i:2 * g + i + 1, 0:T]
                        act.activation(dst, uf[:, i:i + 1, 0:T], ACT.Copy).then_inc(u_hi_ready, 1)

                for g in range(FIRST_ADA):
                    for j in range(4):
                        split_ahead(w0 + 4 * g + j)
                        if j == 3:
                            drain_up(g, g)
                        for step in sum(filter_steps(f, g, j), []):
                            filter_step(f, step)
                with act.Fori(0, ADA_UP // 2) as i:
                    for half in range(2):
                        for j in range(4):
                            split_ahead_in_loop(w0 + 4 * (FIRST_ADA + half), j, 8, i)
                        drain_up(i * 2 + (FIRST_ADA + half), FIRST_ADA + half)
                wd = w0 + 4 * UP_GROUPS
                for half in range(2):
                    with act.Fori(0, DOWN_PAIRS // 4) as i:
                        for j in range(4):
                            split_ahead_in_loop(wd, j, 4, i)
                    for j in range(DOWN_PAIRS // 4 * 4, DOWN_PAIRS):
                        split_ahead(wd + j)
                    wd += DOWN_PAIRS

            def mix(layer):
                T, nc_, S = MIX_T[layer], N_CHUNKS[layer], MIX_T[layer] // SEQ
                w = mix_first[layer]
                small, units = SMALL[layer], UNITS[layer]
                A, B = prm[:, layer, 0:COLS_A], prm[:, layer, COLS_A:]

                def tile_in(name, i):
                    wait_tile(act, layer, name, i)

                for name, _, _, _, pairs, _ in mix_gemms(layer)[:4]:
                    for j in range(pairs):
                        split_ahead(w)
                        w += 1
                    bank0 = 4 * (GEMM_AT[name] % 2)
                    for i in range(in_tiles(layer, name)):
                        if name in ("k", "q"):
                            col = DA if name == "k" else 0
                            tile_in(name, i)
                            act.activation(qk[:, i, col:col + DA], ps[:, bank0 + i, :], ACT.Copy)\
                                .then_inc(drained[layer][name], 1)
                        elif name == "v":
                            tile_in(name, i)
                            act.activation(vtok[:, i, :], ps[:, bank0 + i, :], ACT.Copy).then_inc(drained[layer][name], 1)
                        elif name == "sgv":
                            tile_in(name, i)
                            act.activation(sgv[:, i, :], ps[:, bank0 + i, 0:SGW], ACT.Gelu)\
                                .then_inc(drained[layer][name], 1)

                def drain_features(name):
                    for i in range(4):
                        tile_in(name, i)
                        if name == "f1" and i >= 2:
                            act.activation(sgu[:, i - 2, 0:T], ps[:, i, 0:T], ACT.Gelu)\
                                .then_inc(drained[layer][name], 1)
                        else:
                            c = i if name == "f0" else 4 + i
                            act.activation(u_raw[c][:, 0:T], ps[:, i, 0:T], ACT.Copy).then_inc(drained[layer][name], 1)
                            act.wait_ge(drained[layer][name], i + 1)
                            act.activation(hy[:, c, 0:T], u_raw[c][:, 0:T], ACT.Identity,
                                           bias=B[:, 18 + c:19 + c], scale=B[:, 6 + c:7 + c])\
                                .then_inc(conv_ready[layer], 1)

                def small_in(step):
                    act.wait_ge(small_done[layer], small[step] + 1)
                    return ps[:, 4 + 2 * (small[step] % 2):6 + 2 * (small[step] % 2), :]

                def free(step):
                    return slot_free[layer][small[step] % 2]

                for step in SCHED[layer]:
                    kind = step[0]
                    if kind == "pair":
                        split_ahead(w)
                        w += 1
                    elif kind == "drain":
                        name = step[1]
                        if name[0] == "f":
                            drain_features(name)
                            if name == "f1":
                                for i in range(2):
                                    act.wait_ge(yc_full[layer], i + 1)
                                    act.activation(yc_hi[:, i, 0:T], sgu[:, i, 0:T], ACT.Copy)\
                                        .then_inc(yc_hi_ready[layer], 1)
                        elif name.startswith("gate_"):
                            branch, g = "abc".index(name[5]), int(name[6])
                            for i in range(4):
                                tile_in(name, i)
                                if name == "gate_c0":
                                    act.wait_ge(ws_ready, layer + 1)
                                elif name != "gate_a1":
                                    before = {"gate_c1": "br_c0", "gate_b0": "br_c1", "gate_b1": "br_b0", "gate_a0": "br_b1"}
                                    if before[name][3] == "c":
                                        act.wait_ge(drained[layer][before[name]], i + 1)
                                    else:
                                        act.wait_ge(merged_added, 16 * layer + 4 * (before[name] == "br_b1") + i + 1)
                                col = 96 + branch * KD + g * 4 + i
                                dst = gate_a1 if name == "gate_a1" else gate
                                act.activation(dst[:, i, 0:T], ps[:, i, 0:T], ACT.Sigmoid,
                                               bias=A[:, col:col + 1]).then_inc(drained[layer][name], 1)
                    elif kind == "qk_turn":
                        c, bank = step[1], small_in(step)
                        if c < nc_:
                            act.activation(qT[:, :, c * P:(c + 1) * P], bank[:, 0, :].rearrange("p (h n) -> p h n", h=HEADS),
                                           ACT.Copy)
                        act.activation(kT[:, :, c * P:(c + 1) * P], bank[:, 1, :].rearrange("p (h n) -> p h n", h=HEADS),
                                       ACT.Copy).then_inc(qkT_ready[layer], 1)
                        act.wait_ge(qkT_ready[layer], c + 1)
                        act.sem_inc(free(step), 1)
                    elif kind == "scores":
                        u = step[1]
                        qcs, key0, h = units[u]
                        bank = small_in(step)
                        act.wait_ge(max_ready[layer], u + 1)
                        n = len(qcs)
                        for i in range(2 * n):
                            c, q = i // n, i % n
                            cols = 512 // n
                            ins = act.activation(exps_of(u)[:, c, q * cols:(q + 1) * cols],
                                                 bank[:, c, q * cols:(q + 1) * cols],
                                                 ACT.Exp, bias=sm[:, u % 2, i:i + 1], scale=DH ** -0.5,
                                                 accum_out=sm[:, u % 2, 4 + i:5 + i])
                        ins.then_inc(exp_ready[layer], 1)
                        act.wait_ge(exp_ready[layer], u + 1)
                        act.sem_inc(free(step), 1)
                    elif kind == "turn":
                        u, bank = step[1], small_in(step)
                        if u:
                            act.wait_ge(small_done[layer], small[("mixv", u - 1)] + 1)
                        act.activation(aT[:, :], bank[:, 0, :], ACT.Copy).then_inc(aT_ready[layer], 1)
                        act.wait_ge(aT_ready[layer], u + 1)
                        act.sem_inc(free(step), 1)
                    elif kind == "mixv":
                        u, bank = step[1], small_in(step)
                        qcs, _, h = units[u]
                        for i, qc in enumerate(qcs):
                            act.activation(o_tok[qc][:, h * DV:(h + 1) * DV], bank[:, 0, i * DV:(i + 1) * DV], ACT.Copy)
                            ins = act.activation(aT[:, i * DV:(i + 1) * DV], bank[:, 0, i * DV:(i + 1) * DV], ACT.Square,
                                                 accum_out=head_sq[:, 4 * qc + h:4 * qc + h + 1])
                        ins.then_inc(o_ready[layer], 1)
                        act.wait_ge(o_ready[layer], u + 1)
                        act.sem_inc(free(step), 1)
                    elif kind == "h_turn":
                        bank = small_in(step)
                        n = nc_ * HYW
                        act.activation(htok[:, 0:nc_, :].rearrange("p c n -> p (c n)"),
                                       bank.rearrange("p b n -> p (b n)")[:, 0:n], ACT.Copy)\
                            .then_inc(htok_ready[layer], 1)
                        act.wait_ge(htok_ready[layer], step[1] + 1)
                        act.sem_inc(free(step), 1)
                    elif kind == "h_inv" and step[1] == 1 and step[2] == S - 1:
                        act.wait_ge(yb_full, layer + 1)
                        act.activation(yb_hi[:, :, 0:T], hy[:, 0:2, 0:T], ACT.Copy).then_inc(yb_hi_ready, 1)
                    elif kind == "y_turn":
                        c, bank = step[1], small_in(step)
                        for i in range(2):
                            ins = act.activation(ya_hi[:, :, (2 * c + i) * P:(2 * c + i + 1) * P],
                                                 bank[:, i, :].rearrange("p (h n) -> p h n", h=HEADS),
                                                 ACT.Copy, scale=B[:, 28:29])
                        ins.then_inc(ya_hi_ready[layer], 1)

                for k in range(KD):
                    if k == 0:
                        tile_in("gate_a1", 3)
                    act.wait_ge(merged_added, 16 * layer + 8 + k + 1)
                    act.activation(h_hi[:, k, 0:T], merged[:, k, 0:T], ACT.Copy).then_inc(m_hi_ready[layer], 1)
                for g in range(2):
                    for j in range(4):
                        split_ahead(w)
                        w += 1

            for layer in range(DEPTH):
                norm(3 * layer, TOK, sq_h)
                ffn(2 * layer)
                norm(3 * layer + 1, TOK, sq_h)
                mix(layer)
                norm(3 * layer + 2, MIX_T[layer], sq_m)
                ffn(2 * layer + 1)

            act.wait_ge(out_turned, 4)
            act.activation(y_out[:, 1, 512:D], ps[:, 7, :], ACT.Copy).then_inc(out_copied_a, 1)

        @block.tensor
        def _(pe):
            def transpose(dst, src, rows):
                return pe.transpose(dst, src, ident[0:rows, 0:rows])

            pe.wait_ge(const_loaded, 16)
            pe.wait_ge(c_loaded, 32)
            transpose(ps[:, 6, 0:2 * KD], crow[:, :], 2 * KD).then_inc(c_turned, 1)

            def turn_rows():
                pe.wait_ge(row_cleared, 1)
                pe.wait_ge(x0_ready, 2 * NT)
                pe.wait_ge(row_loaded, 16 * N_ROWS)
                for layer in range(DEPTH):
                    at = layer * (COLS_A + COLS_B)
                    transpose(ps[:, 3, at:at + COLS_A], prow[0:COLS_A, layer, 0, :], COLS_A)
                    ins = transpose(ps[:, 3, at + COLS_A:at + COLS_A + COLS_B], prow[0:COLS_B, layer, 1, :], COLS_B)
                ins.then_inc(turned, 1)

            for c in range(NT):
                pe.wait_ge(raw_loaded[c], 32)
                if c >= 2:
                    pe.wait_ge(x0_ready, 2 * (c - 1))
                for k in range(KD):
                    bank = 2 * (c % 2) + k // 4
                    ins = transpose(ps[:, bank, (k % 4) * P:(k % 4 + 1) * P], raw[:, c, k * P:(k + 1) * P], P)
                ins.then_inc(xt_done, 1)

            def ada0_group(i, q):
                if i == 0:
                    pe.wait_ge(sil_ready, 1)
                pe.wait_ge(ada0_loaded[q], 16)
                for k in range(KD):
                    ins = pe.matmul(ps[0:2, 4 + i, :], sil_c[:, k, :], ada0[:, q, k * 512:(k + 1) * 512],
                                    start=k == 0, stop=k == KD - 1)
                ins.then_inc(rows2_done, 1)

            def turn_rows2(i):
                pe.wait_ge(rows2_out, i + 1)
                for tile in range(4):
                    ins = transpose(ps[:, 4 + i, tile * 2:tile * 2 + 2], rows2[:, i, tile * P:(tile + 1) * P], 2)
                ins.then_inc(ada0_done, 1)

            def fold_sums(bank, acc):
                for tile in range(4):
                    for s in range(2):
                        ins = pe.matmul(ps[:, bank, tile * 2 + s:tile * 2 + s + 1], acc[:, s, tile * P:(tile + 1) * P],
                                        ones[:, 0:1], start=True, stop=True)
                return ins

            def filter_step(layer, step):
                v0, a0 = FLT_V * layer, FLT_A * layer
                if step == 0:
                    pe.wait_ge(flt_loaded, 96 * (layer + 1))
                    pe.wait_ge(h_ready, KD * (2 * layer + 1))
                    ins = pe.matmul(ps[0:FH, MISC, 0:SEQ], fw1[:, :], zt[:, :], start=True, stop=True)
                elif step == 1:
                    pe.wait_ge(flt_a, a0 + 1)
                    ins = pe.matmul(ps[0:FH, MISC, 0:SEQ], fw2[:, :], f_sin[:, 0, :], start=True, stop=True)
                elif step < 6:
                    c, way = (step - 2) // 2, step % 2
                    pe.wait_ge(flt_a, a0 + 2)
                    if step > 2:
                        pe.wait_ge(flt_v, v0 + FLT_V_BEFORE[step])
                    ins = pe.matmul(ps[:, MISC, :], f_sin[:, 1, c * P:(c + 1) * P],
                                    fw3[:, way * 512:(way + 1) * 512], start=True, stop=True)
                elif step == 6:
                    pe.wait_ge(flt_a, a0 + 6)
                    for c in range(2):
                        for way in range(2):
                            ins = pe.matmul(ps[:, MISC, :], ones[:, :], tmag[:, c, way, :],
                                            start=c + way == 0, stop=c + way == 2)
                else:
                    fc, part = (step - 7) // 2, (step - 7) % 2
                    pe.wait_ge(flt_v, v0 + FLT_V_BEFORE[step])
                    for c in range(2):
                        ins = pe.matmul(ps[:, MISC, :], dft_f0[:, c, part, fc * P:(fc + 1) * P],
                                        tmag[:, c, part, :], start=c == 0, stop=c == 1)
                ins.then_inc(flt_pe, 1)

            def norm_sums(n, T, squares):
                nt = T // P
                if n > 0:
                    pe.wait_ge(x_ready, KD * (n - 1) + 4)
                    pe.wait_ge(ada_taken, sum(ADA_FFN_GROUPS[:(2 * n + 1) // 3]))
                for k in (*range(ADDED, KD), 0):
                    if k == 0:
                        pe.wait_ge(squares_added, (ADDED - 1) * (n + 1))
                    else:
                        pe.wait_ge(squared, KD * n + k + 1)
                    for c in range(nt):
                        ins = pe.matmul(ps[:, MISC, c:c + 1], squares[:, k, c * P:(c + 1) * P], ones[:, 0:1],
                                        start=k == ADDED and c == 0, stop=k == 0, skip_group_check=True)
                ins.then_inc(sums_done, 1)

            def keep_warm(count, bank=6):
                for _ in range(count):
                    pe.matmul(ps[:, bank, 0:P], ones[:, :], ident[:, :], start=True, stop=True)

            def norm_spread(n, T):
                for c in range(T // P):
                    pe.wait_ge(diag_ready, NT * n + c + 1)
                    cols = slice(c * P, (c + 1) * P)
                    ins = pe.matmul(ps[:, MISC, cols], ones[:, :], diag[:, cols], start=True, stop=True)
                ins.then_inc(rstd_spread, 1)

            pe.wait_ge(ones_set, 2)
            ada0_group(0, 0)
            norm_sums(0, TOK, sq_h)
            turn_rows()
            ada0_group(1, 1)
            turn_rows2(0)
            norm_spread(0, TOK)
            keep_warm(WARM[1])
            ada0_group(2, 3)
            turn_rows2(1)
            pe.wait_ge(acc0_step, 16)
            pe.wait_ge(mod_step, 1)
            fold_sums(4, acc0).then_inc(ada0_done, 1)
            turn_rows2(2)
            keep_warm(WARM[1], 0)

            def product(out, lhs, rhs, first, last, wait=None):
                if wait is not None:
                    pe.wait_ge(wait[0], wait[2])
                pe.matmul(out, lhs[0], rhs[0], start=first, stop=False)
                crossed = [(lhs[1], rhs[0]), (lhs[0], rhs[1])]
                if wait is not None and wait[3]:
                    crossed.reverse()
                pe.matmul(out, *crossed[0], start=False, stop=False)
                if wait is not None:
                    pe.wait_ge(wait[1], wait[2])
                return pe.matmul(out, *crossed[1], start=False, stop=last)

            def feature_pair(w, offsets, banks, moving, k0, T, first, last, done, before=None, chunk=None):
                slot, tiles = w % SLOTS, len(offsets)
                order = [(m, k) for m in range(tiles) for k in range(2)] if chunk is None else \
                        [(m, k) for k in range(2) for m in range(tiles)]
                for m, k in order:
                    if before is not None and k == 0:
                        before(m)
                    cols = slice(k * 512 + offsets[m], k * 512 + offsets[m] + P)
                    rhs = [v[:, bass.ds(k0 + k, 1), 0:T] if not isinstance(k0, int) else v[:, k0 + k, 0:T]
                           for v in moving]
                    ins = product(ps[:, banks[m], 0:T], (w_hi[:, slot, cols], w_lo[:, slot, cols]), rhs,
                                  first and k == 0, last and k == 1,
                                  chunk(k) if m == 0 and chunk is not None else None)
                    if last and k == 1 and m < tiles - 1:
                        ins.then_inc(done, 1)
                return ins

            H = (h_hi, h_lo)
            U = (u_hi, u_lo)

            def ffn(f):
                layer, sub, T = FFNS[f]
                w0, n = ffn_first[f], 3 * (f // 2) + 2 * (f % 2)
                uf0 = KF * f

                def fold(G):
                    pe.wait_ge(ada_step, G * 16 + 16)
                    if not isinstance(G, int) or G > 0:
                        pe.wait_ge(ada_taken, G)
                    elif f == 0:
                        pe.wait_ge(flt_v, FLT_V)
                    fold_sums(MISC, ada_acc).then_inc(ada_folded, 1)

                def up_group(g, parity, w_at, fold_before):
                    banks = banks_of(parity)

                    def first_pair(m):
                        if m == 3 and not (isinstance(g, int) and g == 0):
                            pe.wait_ge(uf_ready, g * 2 + uf0)
                        if m == 1 and fold_before is not None:
                            fold(fold_before)

                    for j in range(4):
                        middle, after = filter_steps(f, g, j)

                        def steps_in_middle(m):
                            if m == 2:
                                for step in middle:
                                    filter_step(f, step)

                        pe.wait_ge(lo_ready, g * 4 + (w0 + j + 1))

                        def h_made(k):
                            return h_hi_ready, h_ready, KD * n + 2 * j + k + 1, False

                        ins = feature_pair(w_at + j, up_tiles(), banks, H, 2 * j, T, j == 0, j == 3, tile_done[f],
                                           before=first_pair if j == 0 else steps_in_middle,
                                           chunk=h_made if isinstance(g, int) and g == 0 else None)
                        ins.then_inc(pair_used, 1)
                        for step in after:
                            filter_step(f, step)

                groups, G0 = ADA_FFN_GROUPS[f], ADA_FFN_FIRST[f]
                for g in range(FIRST_ADA):
                    up_group(g, g, w0 + 4 * g, None)
                up_group(FIRST_ADA, FIRST_ADA, w0 + 4 * FIRST_ADA, None)
                with pe.Fori(0, (ADA_UP - 2) // 2) as i:
                    for half in range(2):
                        g = FIRST_ADA + 1 + half
                        up_group(i * 2 + g, g, w0 + 4 * g, i * 2 + (G0 + half) if groups else None)
                up_group(UP_GROUPS - 1, UP_GROUPS - 1, w0 + 4 * (UP_GROUPS - 1), G0 + ADA_UP - 2 if groups else None)

                wd = w0 + 4 * UP_GROUPS
                G = G0 + ADA_UP
                for half in range(2):
                    banks = banks_of(UP_GROUPS + half)

                    def first_pair(m):
                        if m == 3:
                            if half == 1:
                                pe.wait_ge(x_ready, KD * n + 4)
                            else:
                                pe.wait_ge(uf_ready, uf0 + KF)
                        if m == 1 and half == 0 and groups:
                            fold(G - 1)

                    def down_pair(w, k0, w_value, u_value, first, last):
                        pe.wait_ge(lo_ready, w_value)
                        if half == 0:
                            pe.wait_ge(u_ready, u_value)
                        ins = feature_pair(w, (0, P, 2 * P, 3 * P), banks, U, k0, T, first, last, tile_done[f],
                                           before=first_pair if first else None)
                        ins.then_inc(pair_used, 1)

                    down_pair(wd, 0, wd + 1, uf0 + 2, True, False)
                    with pe.Fori(0, 2) as i:
                        for j in range(1, 5):
                            down_pair(wd + j, i * 8 + 2 * j, i * 4 + (wd + j + 1), i * 8 + (uf0 + 2 * j + 2), False, False)
                        if ADA_DOWN[f][half]:
                            fold(i + G)
                    G += ADA_DOWN[f][half]
                    for j in range(9, DOWN_PAIRS):
                        if f == len(FFNS) - 1 and half == 1 and j == DOWN_PAIRS - 1:
                            for c in range(2):
                                for k in range(4):
                                    ins = transpose(ps[:, 4 + c, k * P:(k + 1) * P], x[:, k, c * P:(c + 1) * P], P)
                                ins.then_inc(out_turned, 1)
                        down_pair(wd + j, 2 * j, wd + j + 1, uf0 + 2 * j + 2, False, j == DOWN_PAIRS - 1)
                    wd += DOWN_PAIRS

            def mix(layer):
                T, nc_, S = MIX_T[layer], N_CHUNKS[layer], MIX_T[layer] // SEQ
                w = mix_first[layer]
                small = SMALL[layer]
                n = 3 * layer + 1
                done = mix_done[layer]
                gemms = {g[0]: g for g in mix_gemms(layer)}

                def token_pair(name, j, w):
                    cols = gemms[name][5]
                    bank0 = 4 * (GEMM_AT[name] % 2)
                    tiles = in_tiles(layer, name)
                    order = [(i, k) for k in range(2) for i in range(tiles)] if name == "k" else \
                            [(i, k) for i in range(tiles) for k in range(2)]
                    for i, k in order:
                        if j == 0 and k == 0 and GEMM_AT[name] >= 2:
                            before = mix_gemms(layer)[GEMM_AT[name] - 2][0]
                            if i < in_tiles(layer, before):
                                pe.wait_ge(drained[layer][before], i + 1)
                        wait = (h_hi_ready, h_ready, KD * n + 2 * j + k + 1, True) if name == "k" and i == 0 else None
                        lhs = [v[:, 2 * j + k, i * P:(i + 1) * P] for v in H]
                        rhs = [v[:, w % SLOTS, k * 512:k * 512 + cols] for v in (w_hi, w_lo)]
                        ins = product(ps[:, bank0 + i, 0:cols], lhs, rhs, j == 0 and k == 0, j == 3 and k == 1, wait)
                        if j == 3 and k == 1 and i < tiles - 1:
                            ins.then_inc(done, 1)
                    ins.then_inc(pair_used, 1)

                def mix_pair(name, j, w, banks, moving, before, chunk=None):
                    last = j == gemms[name][4] - 1
                    feature_pair(w, (0, P, 2 * P, 3 * P), banks, moving, 2 * j, T, j == 0, last, done,
                                 before=before if j == 0 else None, chunk=chunk).then_inc(pair_used, 1)

                for name in ("k", "q", "v", "sgv"):
                    for j in range(4):
                        pe.wait_ge(lo_ready, w + 1)
                        token_pair(name, j, w)
                        w += 1

                def small_at(step):
                    n = small[step]
                    if n < 2:
                        pe.wait_ge(drained[layer]["sgv"], nc_)
                        pe.wait_ge(drained[layer]["q"], nc_)
                    else:
                        pe.wait_ge(slot_free[layer][n % 2], n // 2)
                    return ps[:, 4 + 2 * (n % 2):6 + 2 * (n % 2), :]

                units = UNITS[layer]
                for step in SCHED[layer]:
                    kind = step[0]
                    if kind == "pair":
                        name, j = step[1:]
                        pe.wait_ge(lo_ready, w + 1)
                        before = "v" if name == "f0" else mix_gemms(layer)[GEMM_AT[name] - 1][0]

                        def tile_drained(m):
                            pe.wait_ge(drained[layer][before], m + 1)

                        if name[0] in "fg":
                            mix_pair(name, j, w, (0, 1, 2, 3), H, tile_drained)
                        else:
                            branch = name[3]
                            if j == 0:
                                pe.wait_ge({"a": ya_ready[layer], "b": yb_ready, "c": yc_ready[layer]}[branch],
                                           {"a": S, "b": layer + 1, "c": 2}[branch])
                            mix_pair(name, j, w, (0, 1, 2, 3),
                                     {"a": (ya_hi, ya_lo), "b": (yb_hi, yb_lo), "c": (yc_hi, yc_lo)}[branch],
                                     tile_drained)
                        w += 1
                        continue
                    if kind in ("drain", "weights", "heads"):
                        continue
                    bank = small_at(step)
                    if kind == "ws_turn":
                        pe.wait_ge(mixc_loaded, 16 * 9 * (layer + 1))
                        for g in range(4):
                            ins = transpose(bank[:, 0, g * P:(g + 1) * P], ws[:, g, :], P)
                    elif kind == "qk_turn":
                        c = step[1]
                        pe.wait_ge(qk_normed[layer], NT + min(c + 1, nc_))
                        for h in range(HEADS):
                            if c < nc_:
                                transpose(bank[:, 0, h * P:(h + 1) * P], qk[:, c, h * P:(h + 1) * P], P)
                            ins = transpose(bank[:, 1, h * P:(h + 1) * P], qk[:, c, DA + h * P:DA + (h + 1) * P], P)
                    elif kind == "sg_mix":
                        pe.wait_ge(ln_done[layer], nc_)
                        pe.wait_ge(ws_ready, layer + 1)
                        for c in range(nc_):
                            for g in range(4):
                                ins = pe.matmul(bank[64 * (g % 2):64 * (g % 2) + 64, g // 2, c * P:(c + 1) * P],
                                                sgv[:, c, g * 64:(g + 1) * 64], wsT[:, g, :], start=True, stop=True)
                    elif kind == "scores":
                        qcs, key0, h = units[step[1]]
                        pe.wait_ge(qkT_ready[layer], 4)
                        cols = 512 // len(qcs)
                        for c in range(2):
                            rows = slice(c * DH, (c + 1) * DH)
                            for i, qc in enumerate(qcs):
                                ins = pe.matmul(bank[:, c, i * cols:(i + 1) * cols], qT[rows, h, qc * P:(qc + 1) * P],
                                                kT[rows, h, key0 * P:key0 * P + cols], start=True, stop=True)
                    elif kind == "turn":
                        pe.wait_ge(a_ready[layer], step[1] + 1)
                        for i in range(4):
                            ins = transpose(bank[:, 0, i * P:(i + 1) * P],
                                            exps_of(step[1])[:, 0, i * P:(i + 1) * P], P)
                    elif kind == "mixv":
                        qcs, key0, h = units[step[1]]
                        pe.wait_ge(aT_ready[layer], step[1] + 1)
                        pe.wait_ge(drained[layer]["v"], 4)
                        n = 4 // len(qcs)
                        for i in range(len(qcs)):
                            for k in range(n):
                                ins = pe.matmul(bank[:, 0, i * DV:(i + 1) * DV], aT[:, (i * n + k) * P:(i * n + k + 1) * P],
                                                vtok[:, key0 + k, h * DV:(h + 1) * DV], start=k == 0, stop=k == n - 1)
                    elif kind == "h_turn":
                        order = step[1]
                        if order == 0:
                            pe.wait_ge(taps_done[layer], 2)
                        else:
                            pe.wait_ge(z_ready[layer], S)
                        for c in range(nc_):
                            for i in range(2):
                                ins = transpose(bank[:, c // 2, (c % 2) * HYW + i * P:(c % 2) * HYW + (i + 1) * P],
                                                hy[:, 2 * order + i, c * P:(c + 1) * P], P)
                    elif kind == "h_fwd":
                        _, order, s = step
                        pe.wait_ge(htok_ready[layer], order + 1)
                        pe.wait_ge(dft_loaded, 16 * 5 * (layer + 1))
                        for part in range(2):
                            for fc in range(2):
                                for c in range(2):
                                    ins = pe.matmul(bank[:, part, fc * HYW:(fc + 1) * HYW],
                                                    dft[:, c, 0, part, fc * P:(fc + 1) * P], htok[:, 2 * s + c, :],
                                                    start=c == 0, stop=c == 1)
                    elif kind == "h_inv":
                        _, order, s = step
                        pe.wait_ge(hprod_ready[layer], order * S + s + 1)
                        for i in range(2):
                            for fc in range(2):
                                for part in range(2):
                                    ins = pe.matmul(bank[:, 0, i * SEQ:(i + 1) * SEQ],
                                                    hprod[:, fc, part, i * P:(i + 1) * P], dft[:, fc, 1, part, :],
                                                    start=fc + part == 0, stop=fc + part == 2)
                    elif kind == "y_turn":
                        c = step[1]
                        pe.wait_ge(o_normed[layer], 2 * c + 2)
                        for i in range(2):
                            for h in range(HEADS):
                                ins = transpose(bank[:, i, h * P:(h + 1) * P], o_tok[2 * c + i][:, h * DV:(h + 1) * DV], P)
                    ins.then_inc(small_done[layer], 1)

                for g in range(2):
                    for j in range(4):
                        pe.wait_ge(lo_ready, w + 1)
                        if j == 0 and g == 0:
                            for b in range(2):
                                pe.wait_ge(slot_free[layer][b], (len(small) + 1 - b) // 2)

                        def before(m):
                            if g == 1:
                                pe.wait_ge(drained[layer]["br_a1"], m + 1)

                        def m_made(k):
                            return m_hi_ready[layer], m_ready[layer], 2 * j + k + 1, False

                        mix_pair(f"o{g}", j, w, tuple(range(4 - 4 * g, 8 - 4 * g)), H, before, m_made if g == 0 else None)
                        w += 1

            def norm(n, T, squares):
                norm_sums(n, T, squares)
                keep_warm(WARM[0])
                norm_spread(n, T)
                keep_warm(WARM[1])

            ffn(0)
            norm(1, TOK, sq_h)
            mix(0)
            norm(2, TOK, sq_m)
            ffn(1)
            norm(3, TOK, sq_h)
            ffn(2)
            norm(4, TOK, sq_h)
            mix(1)
            norm(5, SEQ, sq_m)
            ffn(3)
            for c in range(2):
                for k in range(4, KD):
                    if c == 0:
                        pe.wait_ge(x_ready, KD * 5 + k + 1)
                    ins = transpose(ps[:, 6 + c, (k % 4) * P:(k % 4 + 1) * P], x[:, k, c * P:(c + 1) * P], P)
                ins.then_inc(out_turned, 1)

        @block.vector
        def _(dve):
            chain = Chain(dve, v_step)

            def link(ins):
                chain.step(ins)
                chain.after()

            dve.memset(ms[:, :], 1.0).then_inc(v_step, 1)
            chain.n += 1

            for c in range(NT):
                dve.wait_ge(xt_done, c + 1)
                for i in range(2):
                    dve.tensor_copy(x[:, 4 * i:4 * i + 4, c * P:(c + 1) * P],
                                    ps[:, 2 * (c % 2) + i, :].rearrange("p (k n) -> p k n", k=4)).then_inc(x0_ready, 1)

            def take_parameters():
                dve.wait_ge(turned, 1)
                link(dve.tensor_copy(prm[:, :, :].rearrange("p l c -> p (l c)"),
                                     ps[:, 3, 0:DEPTH * (COLS_A + COLS_B)]))
                chain.step(dve.tensor_copy(ada_bias[:, :].rearrange("p (l c) -> p l c", l=DEPTH),
                                           prm[:, :, 0:N_MOD * KD]))
                for layer in range(DEPTH):
                    col = prm[:, layer, COLS_A + 28:COLS_A + 29]
                    ins = dve.tensor_scalar(col, col, 1.0 - lam_init(layer), None, ALU.mult)
                    link(ins) if layer == 0 else ins.then_inc(prm_ready, 1)
                dve.wait_ge(prm_ready, 1)

            flat_mod = mod[:, :, :, :].rearrange("p l c s -> p (l c) s")

            def partial_sums(acc, src, k, sem, before, first):
                for s in range(2):
                    if first:
                        ins = dve.tensor_scalar(acc[:, s, :], src, sil_c[:, k, s:s + 1], None, ALU.mult)
                    else:
                        dve.wait_ge(sem, before + (s - 1))
                        ins = dve.scalar_tensor_tensor(acc[:, s, :], src, sil_c[:, k, s:s + 1], acc[:, s, :],
                                                       ALU.mult, ALU.add)
                    ins.then_inc(sem, 1)

            def sum_group(q):
                dve.wait_ge(ada0_loaded[q], 16)
                dve.wait_ge(sil_ready, 1)
                for k in range(KD):
                    partial_sums(acc0, ada0[:, q, k * 512:(k + 1) * 512], k, acc0_step, 2 * k, k == 0)

            take_parameters()

            dve.wait_ge(lv_loaded, 16)
            for layer in range(DEPTH):
                pairs = lv[:, layer, :, :].rearrange("p (i j) n -> p i j n", j=2)
                dve.tensor_tensor(pairs[:, :, 0, :], pairs[:, :, 0, :], pairs[:, :, 1, :], ALU.mult).then_inc(lam_v, 1)
                dve.wait_ge(lam_v, 2 * layer + 1)
                dve.tensor_reduce(lsum[:, 2 * layer:2 * layer + 2], pairs[:, :, 0, :], AX.X, ALU.add).then_inc(lam_v, 1)
            MAGIC = 1.5 * 2.0 ** 23
            TURN = (6.28125, 1.9340515136718750e-3, 2.0 * math.pi - 6.28125 - 1.9340515136718750e-3)
            SIN_MAX = 3.1415925

            def filter_step(layer, step):
                v0, p0 = FLT_V * layer, FLT_P * layer
                Bc = prm[:, layer, COLS_A:]
                count = [v0 + FLT_V_BEFORE[step]]

                def flt(ins):
                    count[0] += 1
                    ins.then_inc(flt_v, 1)
                    dve.wait_ge(flt_v, count[0])

                dve.wait_ge(flt_pe, p0 + step + 1)
                if step < 2:
                    flt(dve.tensor_scalar(f_arg[:, :], ps[0:FH, MISC, 0:SEQ], Bc[0:FH, 29 + step:30 + step],
                                          Bc[0:FH, 31:32], ALU.add, ALU.mult))
                    flt(dve.tensor_scalar(f_turns[:, :], f_arg[:, :], 0.5 / math.pi, MAGIC, ALU.mult, ALU.add))
                    flt(dve.tensor_scalar(f_turns[:, :], f_turns[:, :], -MAGIC, None, ALU.add))
                    for part in TURN:
                        flt(dve.scalar_tensor_tensor(f_arg[:, :], f_turns[:, :], -part, f_arg[:, :], ALU.mult, ALU.add))
                    flt(dve.tensor_scalar(f_arg[:, :], f_arg[:, :], SIN_MAX, -SIN_MAX, ALU.min, ALU.max))
                elif step < 6:
                    c, way = (step - 2) // 2, step % 2
                    flt(dve.tensor_tensor(taps[:, c, way, :], ps[:, MISC, :], decay[:, c, way, :], ALU.mult))
                elif step == 6:
                    flt(dve.reciprocal(inv_l1[:, :], ps[:, MISC, :]))
                    flt(dve.tensor_tensor(tmag[:, :, 0, :], taps[:, :, 0, :], taps[:, :, 1, :], ALU.add))
                    flt(dve.tensor_tensor(tmag[:, :, 1, :], taps[:, :, 1, :], taps[:, :, 0, :], ALU.subtract))
                else:
                    fc, part = (step - 7) // 2, (step - 7) % 2
                    flt(dve.tensor_tensor(spec0[:, fc, part, :], ps[:, MISC, :], inv_l1[:, :], ALU.mult))

            def mod_scale(n):
                layer, sub = n // 3, n % 3
                first = 3 * sub * KD
                if n > 0:
                    dve.wait_ge(ada_taken, sum(ADA_FFN_GROUPS[:(2 * n + 1) // 3]))
                scale = mod[:, layer, first + KD:first + 2 * KD, :]
                link(dve.scalar_tensor_tensor(
                    mod_a[:, n, :, :], scale, 1.0,
                    prm[:, layer, 72 + sub * KD:72 + (sub + 1) * KD].unsqueeze(2).broadcast_to([P, KD, 2]),
                    ALU.add, ALU.mult))

            def mod_gate(n):
                layer, sub = n // 3, n % 3
                first = 3 * sub * KD
                link(dve.tensor_scalar(mod_g[:, n, :, :], mod[:, layer, first + 2 * KD:first + 3 * KD, :],
                                       0.5 if sub != 1 else 1.0, None, ALU.mult))

            def norm_scale(n, T, request):
                nt = T // P
                dve.wait_ge(sums_done, n + 1)
                dve.tensor_scalar(ms[:, 0:nt], ps[:, MISC, 0:nt], 1.0 / D, EPS, ALU.mult, ALU.add).then_inc(ms_ready, 1)
                dve.wait_ge(rstd_ready, request + 1)
                for c in range(nt):
                    dve.tensor_scalar(diag[:, c * P:(c + 1) * P], ident[:, :], rstd[:, c:c + 1], None, ALU.mult)\
                        .then_inc(diag_ready, 1)

            def norm_apply(n, T):
                S = T // SEQ
                layer, sub = n // 3, n % 3
                dve.wait_ge(rstd_spread, n + 1)

                def low(k):
                    dve.wait_ge(h_hi_ready, KD * n + k + 1)
                    dve.tensor_tensor(h_lo[:, k, 0:T], hf[:, k % 3, 0:T], h_hi[:, k, 0:T].bitcast(F32),
                                      ALU.subtract).then_inc(h_ready, 1)

                for k in range(KD):
                    if k >= 3:
                        dve.wait_ge(h_ready, KD * n + k - 2)
                    dve.tensor_tensor(hf[:, k % 3, 0:T], x[:, k, 0:T], ps[:, MISC, 0:T], ALU.mult).then_inc(hf_step, 1)
                    dve.wait_ge(hf_step, HF_FULL(n, k) - S)
                    for s in range(S):
                        part = hf[:, k % 3, s * SEQ:(s + 1) * SEQ]
                        dve.tensor_scalar(part, part, mod_a[:, n, k, s:s + 1],
                                          mod[:, layer, 3 * sub * KD + k, s:s + 1], ALU.mult, ALU.add).then_inc(hf_step, 1)
                    if k:
                        low(k - 1)
                low(KD - 1)

            def split_low(slot, cols, hi_value):
                dve.wait_ge(hi_ready, hi_value)
                view = [v.rearrange("p (k n) -> p k n", k=2)[:, :, 0:cols]
                        for v in (w_lo[:, slot, :], raw[:, slot, :], w_hi[:, slot, :].bitcast(F32))]
                dve.tensor_tensor(view[0], view[1], view[2], ALU.subtract).then_inc(lo_ready, 1)

            def split_ahead(w):
                v = w + LOOK
                if v < N_PAIRS:
                    split_low(v % SLOTS, pair_cols(v), v + 1)

            def ffn(f):
                layer, sub, T = FFNS[f]
                w0, n, S = ffn_first[f], 3 * (f // 2) + 2 * (f % 2), FFNS[f][2] // SEQ
                uf0 = KF * f

                groups, G0 = ADA_FFN_GROUPS[f], ADA_FFN_FIRST[f]

                def ada_unit(G, j):
                    dve.wait_ge(ada_loaded[j % 2], G * 32 + 16 * (j // 2 + 1))
                    if j == 0 and not (isinstance(G, int) and G == 0):
                        dve.wait_ge(ada_folded, G)
                    for k in range(2):
                        partial_sums(ada_acc, ada_raw[:, j % 2, k * 512:(k + 1) * 512], 2 * j + k, ada_step,
                                     G * 16 + (4 * j + 2 * k), j + k == 0)

                def ada_take(G):
                    dve.wait_ge(ada_folded, G + 1)
                    q = G + ADA_START
                    at = slice(4 * q, 4 * q + 4) if isinstance(G, int) else bass.ds(q * 4, 4)
                    dve.tensor_tensor(flat_mod[:, at, :], ps[:, MISC, 0:8].rearrange("p (t s) -> p t s", s=2),
                                      ada_bias[:, at].unsqueeze(2).broadcast_to([P, 4, 2]), ALU.add).then_inc(ada_taken, 1)

                def drain_up(g, parity):
                    banks = banks_of(parity)
                    for i in range(2):
                        if i == 0:
                            dve.wait_ge(tile_done[f], g * 3 + 2)
                        else:
                            dve.wait_ge(pair_used, g * 4 + (w0 + 4))
                        dve.wait_ge(sil_a, g * 2 + (uf0 + i + 1))
                        dve.tensor_tensor(uf[:, i, 0:T], uf[:, i, 0:T], ps[:, banks[2 * i + 1], 0:T], ALU.mult)\
                            .then_inc(uf_ready, 1)
                    for i in range(2):
                        dve.wait_ge(u_hi_ready, g * 2 + (uf0 + i + 1))
                        at = slice(2 * g + i, 2 * g + i + 1) if isinstance(g, int) else bass.ds(g * 2 + i, 1)
                        dve.tensor_tensor(u_lo[:, at, 0:T], uf[:, i:i + 1, 0:T], u_hi[:, at, 0:T].bitcast(F32),
                                          ALU.subtract).then_inc(u_ready, 1)

                def split_in_loop(w, turns, i):
                    v = w + LOOK
                    split_low(v % SLOTS, 512, i * turns + (v + 1))

                for g in range(FIRST_ADA):
                    for j in range(4):
                        split_ahead(w0 + 4 * g + j)
                        if j == 3:
                            drain_up(g, g)
                        for step in sum(filter_steps(f, g, j), []):
                            filter_step(f, step)
                with dve.Fori(0, ADA_UP // 2) as i:
                    for half in range(2):
                        g = FIRST_ADA + half
                        for j in range(4):
                            split_in_loop(w0 + 4 * g + j, 8, i)
                            if groups:
                                ada_unit(i * 2 + (G0 + half), j)
                        drain_up(i * 2 + g, g)
                        if groups:
                            ada_take(i * 2 + (G0 + half))

                if groups:
                    dve.wait_ge(ada_taken, G0 + ADA_UP)
                mod_gate(n)

                wd = w0 + 4 * UP_GROUPS
                G = G0 + ADA_UP
                for half in range(2):
                    with dve.Fori(0, DOWN_PAIRS // 4) as i:
                        for j in range(4):
                            split_in_loop(wd + j, 4, i)
                            if ADA_DOWN[f][half]:
                                ada_unit(i + G, j)
                        if ADA_DOWN[f][half]:
                            ada_take(i + G)
                    G += ADA_DOWN[f][half]
                    for j in range(DOWN_PAIRS // 4 * 4, DOWN_PAIRS):
                        split_ahead(wd + j)
                    if f == len(FFNS) - 1 and half == 1:
                        for c in range(2):
                            dve.wait_ge(out_turned, c + 1)
                            dve.tensor_copy(y_out[:, c, 0:512], ps[:, 4 + c, :]).then_inc(out_copied, 1)
                    wd += DOWN_PAIRS
                    banks = banks_of(UP_GROUPS + half)
                    for m in range(4):
                        if m < 3:
                            dve.wait_ge(tile_done[f], 3 * (UP_GROUPS + half) + m + 1)
                        else:
                            dve.wait_ge(pair_used, wd)
                        residual(n, 4 * half + m, banks[m], S)

            def residual(n, k, bank, S):
                for s in range(S):
                    part = x[:, k, s * SEQ:(s + 1) * SEQ]
                    ins = dve.scalar_tensor_tensor(part, ps[:, bank, s * SEQ:(s + 1) * SEQ], mod_g[:, n, k, s:s + 1],
                                                   part, ALU.mult, ALU.add)
                ins.then_inc(x_ready, 1)

            def mix(layer):
                T, nc_, S = MIX_T[layer], N_CHUNKS[layer], MIX_T[layer] // SEQ
                w = mix_first[layer]
                small, units = SMALL[layer], UNITS[layer]
                Bc = prm[:, layer, COLS_A:]
                drain = drained[layer]
                mod_gate(3 * layer + 1)

                def tile_in(name, i):
                    wait_tile(dve, layer, name, i)

                def head_squares(name, c):
                    is_k = name == "k"
                    dve.wait_ge(drain[name], c + 1)
                    chain.after()
                    src = qk[:, c, DA * is_k:DA * is_k + DA]
                    mean = ms[:, 16 * c + 8 * is_k:16 * c + 8 * is_k + 8]
                    link(dve.tensor_tensor(tmp[:, 0:DA], src, src, ALU.mult))
                    link(dve.tensor_reduce(mean, tmp[:, 0:DA].rearrange("p (h n) -> p h n", n=DH), AX.X, ALU.add))
                    dve.tensor_scalar(mean, mean, 1.0 / DH, EPS, ALU.mult, ALU.add).then_inc(ms_ready, 1)

                def head_norm(name, c):
                    is_k = name == "k"
                    if is_k and c == 0:
                        dve.wait_ge(mixc_loaded, 16 * 9 * (layer + 1))
                    dve.wait_ge(rstd_ready, power_request(layer, f"{name}{c}") + 1)
                    part = qk[:, c, DA * is_k:DA * is_k + DA]
                    heads = part.rearrange("p (h n) -> p h n", n=DH)
                    link(dve.tensor_tensor(heads, heads, rstd[:, 16 * c + 8 * is_k:16 * c + 8 * is_k + 8].unsqueeze(2)
                                           .broadcast_to([P, 8, DH]), ALU.mult))
                    ins = dve.tensor_tensor(heads, heads, qk_gain[:, is_k, :].unsqueeze(1).broadcast_to([P, 8, DH]),
                                            ALU.mult)
                    if c >= 2:
                        ins.then_inc(qk_normed[layer], 1)
                        return
                    link(ins)
                    pairs = part.rearrange("p (g a s n) -> p g a s n", a=2, s=2, n=16)
                    cos, sin = [rope[:, c, i, :].rearrange("p (a n) -> p a n", a=2).unsqueeze(1)
                                .broadcast_to([P, 8, 2, 16]) for i in range(2)]
                    t1, t2 = [tmp[:, i * 256:(i + 1) * 256].rearrange("p (g a n) -> p g a n", g=8, a=2) for i in range(2)]
                    x1, x2 = pairs[:, :, :, 0, :], pairs[:, :, :, 1, :]
                    chain.step(dve.tensor_tensor(t1, x1, sin, ALU.mult))
                    chain.step(dve.tensor_tensor(t2, x2, sin, ALU.mult))
                    chain.after(1)
                    chain.step(dve.tensor_tensor(x1, x1, cos, ALU.mult))
                    chain.after(1)
                    chain.step(dve.tensor_tensor(x2, x2, cos, ALU.mult))
                    chain.after(1)
                    link(dve.tensor_tensor(x1, x1, t2, ALU.subtract))
                    dve.tensor_tensor(x2, x2, t1, ALU.add).then_inc(qk_normed[layer], 1)
                    dve.wait_ge(qk_normed[layer], NT * (not is_k) + c + 1)

                def ln_stats(c):
                    if c == 0:
                        dve.wait_ge(drain["sgv"], nc_)
                    link(dve.bn_stats(stats[:, c, 0:6], sgv[:, c, :]))
                    chain.step(dve.bn_aggr(stats[:, c, 6:8], stats[:, c, 0:6]))
                    if c == nc_ - 1:
                        chain.after()
                        dve.tensor_scalar(ms[:, 0:nc_], stats[:, 0:nc_, 7], EPS, None, ALU.add).then_inc(ms_ready, 1)

                def ln_apply(c):
                    if c == 0:
                        dve.wait_ge(rstd_ready, power_request(layer, "ln") + 1)
                    part = sgv[:, c, :]
                    link(dve.tensor_scalar(part, part, stats[:, c, 6:7], rstd[:, c:c + 1], ALU.subtract, ALU.mult))
                    link(dve.tensor_tensor(part, part, ln_g[:, :], ALU.mult))
                    dve.tensor_tensor(part, part, ln_b[:, :], ALU.add).then_inc(ln_done[layer], 1)

                def each_chunk(step):
                    for c in range(nc_):
                        step(c)

                def outer_taps(c):
                    dve.wait_ge(conv_ready[layer], c + 1)
                    for tap, to, of in ((0, slice(1, SEQ), slice(0, SEQ - 1)), (2, slice(0, SEQ - 1), slice(1, SEQ))):
                        dst, src = [v.rearrange("p (s n) -> p s n", s=S)[:, :, cut]
                                    for v, cut in ((hy[:, c, 0:T], to), (u_raw[c][:, 0:T], of))]
                        ins = dve.scalar_tensor_tensor(dst, src, Bc[:, 6 * tap + c:6 * tap + c + 1], dst,
                                                       ALU.mult, ALU.add)
                        if tap == 0:
                            link(ins)
                    ins.then_inc(taps_done[layer], 1)

                extras = {("f0", 2): [(each_chunk, ln_stats)], ("f0", 3): [(each_chunk, ln_apply)]}
                for c, at in enumerate((("f1", 0), ("f1", 1), ("f1", 2), ("f1", 3), ("gate_c0", 0), ("gate_c0", 1))):
                    extras[at] = [(outer_taps, c)]
                for c in range(NT):
                    extras["q", c] = [(head_squares, "k", c)]
                    extras["v", c] = [(head_norm, "k", c)]
                for c in range(nc_):
                    extras["v", c] += [(head_squares, "q", c)]
                    extras[(("sgv", 1), ("sgv", 3), ("f0", 0), ("f0", 1))[c]] = [(head_norm, "q", c)]
                for name in ("k", "q", "v", "sgv"):
                    for j in range(4):
                        split_ahead(w)
                        w += 1
                        for what, *args in extras.get((name, j), []):
                            what(*args)
                    bank0 = 4 * (GEMM_AT[name] % 2)

                def gate_spatial():
                    for i in range(2):
                        if i == 0:
                            dve.wait_ge(drain["f1"], 4)
                            chain.after()
                        dve.tensor_tensor(sgu[:, i, 0:T], sgm[:, i, 0:T], sgu[:, i, 0:T], ALU.mult)\
                            .then_inc(yc_full[layer], 1)
                    for i in range(2):
                        dve.wait_ge(yc_hi_ready[layer], i + 1)
                        dve.tensor_tensor(yc_lo[:, i, 0:T], sgu[:, i, 0:T], yc_hi[:, i, 0:T].bitcast(F32),
                                          ALU.subtract).then_inc(yc_ready[layer], 1)

                def small_in(step):
                    dve.wait_ge(small_done[layer], small[step] + 1)
                    return ps[:, 4 + 2 * (small[step] % 2):6 + 2 * (small[step] % 2), :]

                def free(step):
                    return slot_free[layer][small[step] % 2]

                for step in SCHED[layer]:
                    kind = step[0]
                    if kind == "pair":
                        split_ahead(w)
                        w += 1
                        for what, *args in extras.get(step[1:], []):
                            what(*args)
                    elif step == ("drain", "f1"):
                        gate_spatial()
                    elif kind == "drain" and step[1].startswith("br_"):
                        name = step[1]
                        branch, g = name[3], int(name[4])
                        for i in range(4):
                            dve.wait_ge(drain["gate_" + name[3:]], i + 1)
                            tile_in(name, i)
                            part = merged[:, 4 * g + i, 0:T]
                            gated = (gate_a1 if name == "br_a1" else gate)[:, i, 0:T]
                            if branch == "c":
                                dve.tensor_tensor(part, gated, ps[:, i, 0:T], ALU.mult).then_inc(drain[name], 1)
                            else:
                                dve.tensor_tensor(gated, gated, ps[:, i, 0:T], ALU.mult).then_inc(drain[name], 1)
                    elif kind == "ws_turn":
                        bank = small_in(step)
                        dve.tensor_copy(wsT[:, :, :].rearrange("p g n -> p (g n)"), bank[:, 0, :]).then_inc(ws_ready, 1)
                        dve.wait_ge(ws_ready, layer + 1)
                        dve.sem_inc(free(step), 1)
                    elif kind == "sg_mix":
                        bank = small_in(step)
                        for i in range(2):
                            ins = dve.tensor_tensor(sgm[:, i, 0:T].rearrange("p (c n) -> p c n", n=P),
                                                    bank[:, i, 0:T].rearrange("p (c n) -> p c n", n=P),
                                                    sgb[:, i, :].unsqueeze(1).broadcast_to([P, nc_, P]), ALU.add)
                            chain.step(ins)
                        chain.after()
                        dve.sem_inc(free(step), 1)
                    elif kind == "scores":
                        u, bank = step[1], small_in(step)
                        n = 2 * len(units[u][0])
                        largest = sm[:, u % 2, 0:n]
                        link(dve.tensor_reduce(largest, bank.rearrange("p b (i n) -> p (b i) n", i=n // 2),
                                               AX.X, ALU.max))
                        dve.tensor_scalar(largest, largest, -DH ** -0.5, None, ALU.mult).then_inc(max_ready[layer], 1)
                    elif kind == "weights":
                        u = step[1]
                        m = len(units[u][0])
                        dve.wait_ge(exp_ready[layer], u + 1)
                        ex, su = exps_of(u), sm[:, u % 2, :]
                        link(dve.reciprocal(su[:, 8:8 + 2 * m], su[:, 4:4 + 2 * m]))
                        link(dve.tensor_scalar(su[:, 8 + m:8 + 2 * m], su[:, 8 + m:8 + 2 * m], lam[:, layer:layer + 1],
                                               None, ALU.mult))
                        cols = 512 // m
                        for i in range(m):
                            at = slice(i * cols, (i + 1) * cols)
                            chain.step(dve.tensor_scalar(ex[:, 1, at], ex[:, 1, at], su[:, 8 + m + i:9 + m + i],
                                                         None, ALU.mult))
                        for i in range(m):
                            at = slice(i * cols, (i + 1) * cols)
                            chain.after(m - 1 if i == 0 else 0)
                            ins = dve.scalar_tensor_tensor(ex[:, 0, at], ex[:, 0, at], su[:, 8 + i:9 + i], ex[:, 1, at],
                                                           ALU.mult, ALU.add)
                            if i == m - 1:
                                ins.then_inc(a_ready[layer], 1)
                            else:
                                chain.step(ins)
                    elif kind == "h_fwd":
                        _, order, s = step
                        bank = small_in(step)
                        if order == 0 and s == 0:
                            dve.wait_ge(dft_loaded, 16 * 5 * (layer + 1))
                        if order * S + s:
                            last = ("h_inv", order, s - 1) if s else ("h_inv", 0, S - 1)
                            dve.wait_ge(small_done[layer], small[last] + 1)
                        re, im = [bank[:, i, :].rearrange("p (f n) -> p f n", f=2) for i in range(2)]
                        h_re, h_im = [spec[:, :, i, order * HYW:(order + 1) * HYW] for i in range(2)]
                        link(dve.tensor_tensor(htmp[:, :, :], im, h_im, ALU.mult))
                        link(dve.tensor_tensor(hprod[:, :, 0, :], re, h_re, ALU.mult))
                        link(dve.tensor_tensor(hprod[:, :, 0, :], hprod[:, :, 0, :], htmp[:, :, :], ALU.add))
                        link(dve.tensor_tensor(htmp[:, :, :], re, h_im, ALU.mult))
                        link(dve.tensor_tensor(hprod[:, :, 1, :], im, h_re, ALU.mult))
                        dve.sem_inc(free(step), 1)
                        dve.tensor_tensor(hprod[:, :, 1, :], hprod[:, :, 1, :], htmp[:, :, :], ALU.subtract)\
                            .then_inc(hprod_ready[layer], 1)
                    elif kind == "h_inv":
                        _, order, s = step
                        bank = small_in(step)
                        at = slice(s * SEQ, (s + 1) * SEQ)
                        for i in range(2):
                            skip = Bc[:, 24 + 2 * order + i:25 + 2 * order + i]
                            link(dve.scalar_tensor_tensor(htmp[:, i, :], hy[:, 2 * order + i, at], skip,
                                                          bank[:, 0, i * SEQ:(i + 1) * SEQ], ALU.mult, ALU.add))
                        dve.sem_inc(free(step), 1)
                        for i in range(2):
                            dst = hy[:, 2 + i, at] if order == 0 else hy[:, i, at]
                            ins = dve.tensor_tensor(dst, htmp[:, i, :], hy[:, 2 + 2 * order + i, at], ALU.mult)
                            if i == 1 and order == 0:
                                ins.then_inc(z_ready[layer], 1)
                                dve.wait_ge(z_ready[layer], s + 1)
                            elif i == 1 and s == S - 1:
                                ins.then_inc(yb_full, 1)
                            else:
                                chain.step(ins)
                        if order == 1:
                            chain.after()
                        if order == 1 and s == S - 1:
                            dve.wait_ge(yb_hi_ready, layer + 1)
                            dve.tensor_tensor(yb_lo[:, :, 0:T], hy[:, 0:2, 0:T], yb_hi[:, :, 0:T].bitcast(F32),
                                              ALU.subtract).then_inc(yb_ready, 1)
                    elif kind == "heads":
                        c = step[1]
                        dve.wait_ge(o_ready[layer], 8 if c == 0 else len(units))
                        dve.tensor_scalar(ms[:, 0:8], head_sq[:, 8 * c:8 * c + 8], 1.0 / DV, EPS, ALU.mult, ALU.add)\
                            .then_inc(ms_ready, 1)
                        dve.wait_ge(rstd_ready, power_request(layer, f"head{c}") + 1)
                        for i in range(2):
                            part = o_tok[2 * c + i][:, :].rearrange("p (h n) -> p h n", n=DV)
                            dve.tensor_tensor(part, part, rstd[:, 4 * i:4 * i + 4].unsqueeze(2)
                                              .broadcast_to([P, HEADS, DV]), ALU.mult).then_inc(o_normed[layer], 1)
                    elif kind == "y_turn":
                        c, bank = step[1], small_in(step)
                        dve.wait_ge(ya_hi_ready[layer], c + 1)
                        for i in range(2):
                            at = slice((2 * c + i) * P, (2 * c + i + 1) * P)
                            ins = dve.scalar_tensor_tensor(ya_lo[:, :, at],
                                                           bank[:, i, :].rearrange("p (h n) -> p h n", h=HEADS),
                                                           Bc[:, 28:29], ya_hi[:, :, at].bitcast(F32),
                                                           ALU.mult, ALU.subtract)
                            if i == 0:
                                chain.step(ins)
                        ins.then_inc(ya_ready[layer], 1)
                        dve.wait_ge(ya_ready[layer], c + 1)
                        dve.sem_inc(free(step), 1)

                for k in range(KD):
                    dve.wait_ge(m_hi_ready[layer], k + 1)
                    dve.tensor_tensor(h_lo[:, k, 0:T], merged[:, k, 0:T], h_hi[:, k, 0:T].bitcast(F32),
                                      ALU.subtract).then_inc(m_ready[layer], 1)
                for g in range(2):
                    for j in range(4):
                        split_ahead(w)
                        w += 1
                    for m in range(4):
                        tile_in(f"o{g}", m)
                        residual(3 * layer + 1, 4 * g + m, 4 - 4 * g + m, S)

            def take_group(q, bank):
                dve.tensor_tensor(flat_mod[:, 4 * q:4 * q + 4, :], ps[:, bank, 0:8].rearrange("p (t s) -> p t s", s=2),
                                  ada_bias[:, 4 * q:4 * q + 4].unsqueeze(2).broadcast_to([P, 4, 2]), ALU.add)\
                    .then_inc(mod_step, 1)

            dve.wait_ge(lam_a, 1)
            for layer in range(DEPTH):
                dve.scalar_tensor_tensor(lam[:, layer:layer + 1], lsum[:, 2 * layer + 1:2 * layer + 2],
                                         -lam_init(layer), lsum[:, 2 * layer:2 * layer + 1],
                                         ALU.add, ALU.subtract).then_inc(v_step, 1)
                chain.n += 1

            norm_scale(0, TOK, power_request(0, "ffn_a"))
            sum_group(2)
            for v in range(LOOK):
                split_low(v % SLOTS, 512, v + 1)
            for n, (q, bank) in enumerate(((0, 4), (1, 5), (2, 4), (3, 6))):
                dve.wait_ge(ada0_done, n + 1)
                take_group(q, bank)
            dve.wait_ge(mod_step, ADA_START)

            def norm(n, T, request):
                norm_scale(n, T, request)
                norm_apply(n, T)

            mod_scale(0)
            norm_apply(0, TOK)
            for layer in range(DEPTH):
                if layer:
                    mod_scale(3)
                    norm(3, TOK, power_request(layer, "ffn_a"))
                ffn(2 * layer)
                mod_scale(3 * layer + 1)
                norm(3 * layer + 1, TOK, power_request(layer, "mix"))
                mix(layer)
                mod_scale(3 * layer + 2)
                norm(3 * layer + 2, MIX_T[layer], power_request(layer, "ffn_b"))
                ffn(2 * layer + 1)
            dve.wait_ge(out_turned, 3)
            dve.tensor_copy(y_out[:, 0, 512:D], ps[:, 6, :]).then_inc(out_copied, 1)



NAMES = ["x", "c", "ctx", "c_ctx", "ada_w", "ada_b", "norm_g", "ffn_up", "ffn_down", "w_in", "da_qk_gain", "da_lambda",
         "da_subln", "hy_conv_w", "hy_conv_b", "hy_f_w1", "hy_f_b1", "hy_f_w2", "hy_f_b2", "hy_f_freq", "hy_f_w3",
         "hy_skip", "sg_ln_g", "sg_ln_b", "sg_w", "sg_b", "gate_w", "gate_b", "w_br", "w_o"]


def shape_constants():
    n = SEQ
    f32 = np.float32
    time = np.linspace(0.0, 1.0, n)[:, None]
    w = (2.0 * math.pi / n) * np.arange(n)[:, None]
    bands = np.linspace(1e-4, (EMB - 1) // 2 - 1, (EMB - 1) // 2)
    pos = np.concatenate([time, np.cos(bands * w), -np.sin(bands * w)], axis=-1).T
    deltas = np.linspace(math.log(1e-2) / 1.5, math.log(1e-2) / 0.3, 2 * HYW)
    decay = np.repeat(np.exp(-time * np.abs(deltas))[:, None, :], 2, axis=1)
    decay[0, 1] = 0.0
    angle = (2.0 * math.pi / (2 * n)) * np.outer(np.arange(n), np.arange(n) + 0.5)
    fwd = np.stack([np.cos(angle), np.sin(angle)], axis=1)
    inv = np.stack([np.cos(angle).T, np.sin(angle).T], axis=1) / n
    inv_f = 10000.0 ** (-np.arange(16) / 16)
    at = np.arange(n)
    ang = (np.stack([at // GRID_W, at % GRID_W], axis=-1)[:, :, None] * inv_f).reshape(n, 32)
    return {"filter_pos": pos.astype(f32), "decay": decay.astype(f32), "dft": np.stack([fwd, inv]).astype(f32),
            "rope": np.stack([np.cos(ang), np.sin(ang)], axis=1).astype(f32), "ident": np.eye(P, dtype=f32)}


def kernel(**inputs):
    import concourse.bacc as bacc
    from concourse.bass_utils import run_bass_kernel_spmd
    arrays = {name: np.ascontiguousarray(inputs[name]) for name in NAMES} | shape_constants()
    nc = bacc.Bacc("TRN2", target_bir_lowering=False, num_devices=1)
    t = {name: nc.dram_tensor(f"in_{name}", a.shape, F32, kind="ExternalInput").ap() for name, a in arrays.items()}
    out = nc.dram_tensor("out_0", (SEQ, D), F32, kind="ExternalOutput").ap()
    build(nc, t, out)
    r = run_bass_kernel_spmd(nc, [{f"in_{name}": a for name, a in arrays.items()}], core_ids=[0])
    return r.results[0]["out_0"].reshape(1, SEQ, D)
```
